# Optimizing a Trainium2 kernel written in Bass

```python
import math
import jax, jax.numpy as jnp
from jax import lax
import numpy as np

D_MODEL = 1024
BATCH = 1
SEQ = 512
DEPTH = 2

GRID_W = 64
CTX_LEN = 256
N_MIXERS = 4
EPS = 1e-6
ROPE_BASE = 10000.0

FOURIER_GROUPS = 8
DIFF_HEADS = 8
DIFF_HEAD_DIM = 64
DIFF_Q_BLOCK = 128
SSD_D_INNER = 2 * D_MODEL
SSD_HEAD_DIM = 64
SSD_HEADS = SSD_D_INNER // SSD_HEAD_DIM
SSD_STATE = 128
SSD_GROUPS = 8
SSD_CONV = 5
SSD_CONV_DIM = SSD_D_INNER + 2 * SSD_GROUPS * SSD_STATE
SSD_IN_DIM = SSD_D_INNER + SSD_CONV_DIM + 2 * SSD_HEADS
HGRN_HEAD_DIM = 128
HGRN_HEADS = D_MODEL // HGRN_HEAD_DIM
SCAN_CHUNK = 64
PEER_HEADS = 8
PEER_N_KEYS = 128
PEER_EXPERTS = PEER_N_KEYS ** 2
PEER_KEY_DIM = 256
PEER_TOPK = 16
PEER_BLOCK = 128

kernel_name = "hybrid_prefix_dit_fnet_diffattn_ssd_hgrn2_peer"

def rmsnorm(x, g):
    xf = x.astype(jnp.float32)
    y = xf * lax.rsqrt(jnp.mean(xf * xf, -1, keepdims=True) + EPS)
    return (y * g.astype(jnp.float32)).astype(x.dtype)

def group_rmsnorm(x, g, groups):
    shp = x.shape
    xf = x.astype(jnp.float32).reshape(*shp[:-1], groups, shp[-1] // groups)
    xf = xf * lax.rsqrt(jnp.mean(xf * xf, -1, keepdims=True) + EPS)
    return (xf.reshape(shp) * g.astype(jnp.float32)).astype(x.dtype)

def modulate(h, shift, scale):
    return h * (1 + scale) + shift

def axial_rope_tables(length, head_dim):
    rows = length // GRID_W
    row = jnp.repeat(jnp.arange(rows), GRID_W).astype(jnp.float32)
    col = jnp.tile(jnp.arange(GRID_W), rows).astype(jnp.float32)
    nf = head_dim // 4
    freqs = ROPE_BASE ** (-jnp.arange(nf, dtype=jnp.float32) / nf)
    ang = jnp.stack([row[:, None] * freqs, col[:, None] * freqs], axis=1)
    return jnp.cos(ang), jnp.sin(ang)

def apply_axial_rope(x, cos, sin):
    shp = x.shape
    nf = shp[-1] // 4
    xr = x.astype(jnp.float32).reshape(*shp[:-1], 2, 2, nf)
    bshape = (shp[1],) + (1,) * (x.ndim - 3) + (2, nf)
    c, s = cos.reshape(bshape), sin.reshape(bshape)
    xa, xb = xr[..., 0, :], xr[..., 1, :]
    out = jnp.stack([xa * c - xb * s, xb * c + xa * s], axis=-2)
    return out.reshape(shp).astype(x.dtype)

def depthwise_conv_centred(x, w, b):
    pad = (w.shape[0] - 1) // 2
    y = lax.conv_general_dilated(x, w[:, None, :].astype(x.dtype), window_strides=(1,),
                                 padding=[(pad, pad)], dimension_numbers=('NWC', 'WIO', 'NWC'),
                                 feature_group_count=x.shape[-1])
    return y + b

def chunked_gated_scan(q, k, v, log_f, s0, with_output):
    B, L, H, K = k.shape
    V = v.shape[-1]
    Q = SCAN_CHUNK
    nc = L // Q

    def chunks(a):
        return a.reshape(B, nc, Q, *a.shape[2:]).swapaxes(0, 1)

    causal = jnp.tril(jnp.ones((Q, Q), bool))
    scalar_decay = log_f.shape[-1] == 1

    def body(S, inp):
        qc, kc, vc, gc = inp
        cs = jnp.cumsum(gc.astype(jnp.float32), axis=1)
        last = cs[:, -1]
        k_to_end = kc * jnp.exp(last[:, None] - cs)
        S_new = jnp.exp(last)[..., None] * S + jnp.einsum('bjhk,bjhv->bhkv', k_to_end, vc)
        if not with_output:
            return S_new, None
        seg = cs[:, :, None] - cs[:, None, :]
        decay = jnp.exp(jnp.where(causal[None, :, :, None, None], seg, -jnp.inf))
        if scalar_decay:
            w = jnp.einsum('bihk,bjhk->bijh', qc, kc) * decay[..., 0]
        else:
            w = jnp.einsum('bihk,bjhk,bijhk->bijh', qc, kc, decay)
        o = (jnp.einsum('bijh,bjhv->bihv', w, vc)
             + jnp.einsum('bihk,bhkv->bihv', qc * jnp.exp(cs), S))
        return S_new, o

    s_end, o = lax.scan(body, s0, (chunks(q), chunks(k), chunks(v), chunks(log_f)))
    if with_output:
        o = o.swapaxes(0, 1).reshape(B, L, H, V)
    return s_end, o

def context_then_latent_scan(ctx_in, lat_in, reverse, ctx_out):
    flip = (lambda a: jnp.flip(a, axis=1)) if reverse else (lambda a: a)
    qc, kc, vc, gc = [flip(a) for a in ctx_in]
    ql, kl, vl, gl = [flip(a) for a in lat_in]
    B, _, H, K = kc.shape
    s0 = jnp.zeros((B, H, K, vc.shape[-1]), jnp.float32)
    s_ctx, oc = chunked_gated_scan(qc, kc, vc, gc, s0, ctx_out)
    _, ol = chunked_gated_scan(ql, kl, vl, gl, s_ctx, True)
    return (flip(oc) if ctx_out else None), flip(ol)

def fourier_mixer(hc, hl, w_out, ctx_out):
    def mix(h):
        B, L, _ = h.shape
        hg = h.astype(jnp.float32).reshape(B, L, FOURIER_GROUPS, D_MODEL // FOURIER_GROUPS)
        f = jnp.fft.fft2(hg, axes=(1, 3), norm='ortho').real
        return f.reshape(B, L, D_MODEL).astype(h.dtype) @ w_out
    return (mix(hc) if ctx_out else None), mix(hl)

def diff_attention_mixer(hc, hl, w_in, lam, sub_g, w_out, depth_idx, ctx_out):
    H, Dh = DIFF_HEADS, DIFF_HEAD_DIM
    lam_init = 0.8 - 0.6 * math.exp(-0.3 * depth_idx)
    lamf = lam.astype(jnp.float32)
    lam_full = jnp.exp(jnp.sum(lamf[0] * lamf[1])) - jnp.exp(jnp.sum(lamf[2] * lamf[3])) + lam_init
    scale = Dh ** -0.5

    def proj(h):
        B, L, _ = h.shape
        q, k, v = jnp.split(h @ w_in, 3, axis=-1)
        return (q.reshape(B, L, H, 2, Dh) * scale, k.reshape(B, L, H, 2, Dh), v.reshape(B, L, H, 2 * Dh))

    qc, kc, vc = proj(hc)
    ql, kl, vl = proj(hl)
    B, L = hl.shape[:2]
    cos, sin = axial_rope_tables(L, Dh)
    ql, kl = apply_axial_rope(ql, cos, sin), apply_axial_rope(kl, cos, sin)
    keys = jnp.concatenate([kl, kc], axis=1)
    vals = jnp.concatenate([vl, vc], axis=1)

    def attend(q, k, v):
        s = jnp.einsum('bqhcd,bkhcd->bhcqk', q, k).astype(jnp.float32)
        p = jax.nn.softmax(s, axis=-1)
        a = p[:, :, 0] - lam_full * p[:, :, 1]
        return jnp.einsum('bhqk,bkhv->bqhv', a.astype(v.dtype), v)

    nb = L // DIFF_Q_BLOCK
    qb = ql.reshape(B, nb, DIFF_Q_BLOCK, H, 2, Dh).swapaxes(0, 1)
    ob = lax.map(lambda q: attend(q, keys, vals), qb)
    ol = ob.swapaxes(0, 1).reshape(B, L, H, 2 * Dh)

    def finish(o):
        o = rmsnorm(o, sub_g) * (1 - lam_init)
        return o.reshape(*o.shape[:2], H * 2 * Dh) @ w_out

    return (finish(attend(qc, kc, vc)) if ctx_out else None), finish(ol)

def ssd_mixer(hc, hl, w_in, conv_w, conv_b, a_log, dt_bias, d_skip, norm_g, w_out, ctx_out):
    a = -jnp.exp(a_log.astype(jnp.float32))
    rep = SSD_HEADS // SSD_GROUPS

    def project(h):
        B, L, _ = h.shape
        z, xbc, dt = jnp.split(h @ w_in, [SSD_D_INNER, SSD_D_INNER + SSD_CONV_DIM], axis=-1)
        xbc = jax.nn.silu(depthwise_conv_centred(xbc, conv_w, conv_b))
        xs, bm, cm = jnp.split(xbc, [SSD_D_INNER, SSD_D_INNER + SSD_GROUPS * SSD_STATE], axis=-1)
        xs = xs.reshape(B, L, SSD_HEADS, SSD_HEAD_DIM)
        bm = jnp.repeat(bm.reshape(B, L, SSD_GROUPS, SSD_STATE), rep, axis=2)
        cm = jnp.repeat(cm.reshape(B, L, SSD_GROUPS, SSD_STATE), rep, axis=2)
        dt = jax.nn.softplus(dt.astype(jnp.float32).reshape(B, L, 2, SSD_HEADS) + dt_bias.astype(jnp.float32))
        dirs = [(cm, bm * dt[:, :, d, :, None], xs, (dt[:, :, d] * a[d])[..., None]) for d in range(2)]
        return z, xs, dirs

    zc, xsc, dirs_c = project(hc)
    zl, xsl, dirs_l = project(hl)
    oc_f, ol_f = context_then_latent_scan(dirs_c[0], dirs_l[0], False, ctx_out)
    oc_b, ol_b = context_then_latent_scan(dirs_c[1], dirs_l[1], True, ctx_out)

    def finish(o, xs, z):
        B, L = o.shape[:2]
        y = o + xs.astype(jnp.float32) * d_skip.astype(jnp.float32)[:, None]
        y = y.reshape(B, L, SSD_D_INNER).astype(z.dtype)
        y = group_rmsnorm(y * jax.nn.silu(z), norm_g, SSD_GROUPS)
        return y @ w_out

    yc = finish(oc_f + oc_b, xsc, zc) if ctx_out else None
    return yc, finish(ol_f + ol_b, xsl, zl)

def hgrn2_mixer(hc, hl, w_in, lb, norm_g, w_out, ctx_out):
    lbh = lb.reshape(HGRN_HEADS, HGRN_HEAD_DIM)

    def project(h):
        B, L, _ = h.shape
        q, f_fw, f_bw, i_, g = jnp.split(h @ w_in, 5, axis=-1)
        heads = lambda t: t.reshape(B, L, HGRN_HEADS, HGRN_HEAD_DIM)
        q, v = heads(jax.nn.silu(q)), heads(i_)
        dirs = []
        for f_raw in (f_fw, f_bw):
            f = lbh + (1 - lbh) * jax.nn.sigmoid(heads(f_raw).astype(jnp.float32))
            dirs.append((q, 1 - f, v, jnp.log(f)))
        return g, dirs

    gc, dirs_c = project(hc)
    gl, dirs_l = project(hl)
    oc_f, ol_f = context_then_latent_scan(dirs_c[0], dirs_l[0], False, ctx_out)
    oc_b, ol_b = context_then_latent_scan(dirs_c[1], dirs_l[1], True, ctx_out)

    def finish(o, g):
        B, L = o.shape[:2]
        o = group_rmsnorm(o.reshape(B, L, D_MODEL).astype(g.dtype), norm_g, HGRN_HEADS)
        return (o * jax.nn.silu(g)) @ w_out

    yc = finish(oc_f + oc_b, gc) if ctx_out else None
    return yc, finish(ol_f + ol_b, gl)

def peer_ffn(h, w_q, keys, u, v):
    T, D = h.shape
    q = (h @ w_q).reshape(T, PEER_HEADS, 2, PEER_KEY_DIM // 2)
    s = jnp.einsum('thcd,hcnd->thcn', q, keys).astype(jnp.float32)
    sv, si = lax.top_k(s, PEER_TOPK)
    cand = sv[:, :, 0, :, None] + sv[:, :, 1, None, :]
    best, pos = lax.top_k(cand.reshape(T, PEER_HEADS, PEER_TOPK * PEER_TOPK), PEER_TOPK)
    idx1 = jnp.take_along_axis(si[:, :, 0], pos // PEER_TOPK, axis=-1)
    idx2 = jnp.take_along_axis(si[:, :, 1], pos % PEER_TOPK, axis=-1)
    expert = (idx1 * PEER_N_KEYS + idx2).reshape(T, PEER_HEADS * PEER_TOPK)
    gate = jax.nn.softmax(best, axis=-1).reshape(T, PEER_HEADS * PEER_TOPK)
    nb = T // PEER_BLOCK

    def block(args):
        hb, eb, gb = args
        act = jax.nn.gelu(jnp.einsum('tkd,td->tk', u[eb], hb), approximate=False)
        return jnp.einsum('tk,tkd->td', (gb * act).astype(hb.dtype), v[eb])

    out = lax.map(block, (h.reshape(nb, PEER_BLOCK, D), expert.reshape(nb, PEER_BLOCK, -1),
                          gate.reshape(nb, PEER_BLOCK, -1)))
    return out.reshape(T, D)

def setup_inputs(seed: int = 0) -> dict:
    key = jax.random.key(seed)
    ks = iter(jax.random.split(key, 40))
    D = D_MODEL

    def nrm(shape, scale):
        return jax.random.normal(next(ks), shape, jnp.float32) * scale

    def n_of(kind):
        return len(range(kind, DEPTH, N_MIXERS))

    nA, nB, nC, nD = n_of(0), n_of(1), n_of(2), n_of(3)
    dt0 = jnp.exp(jax.random.uniform(next(ks), (nC, 2, SSD_HEADS), jnp.float32,
                                     math.log(1e-3), math.log(1e-1)))
    return {
        "x": nrm((BATCH, SEQ, D), 1.0),
        "c": nrm((BATCH, D), 1.0),
        "ctx": nrm((BATCH, CTX_LEN, D), 1.0),
        "c_ctx": nrm((D,), 1.0),
        "w_mod": nrm((DEPTH, D, 6 * D), 0.5 * D ** -0.5),
        "b_mod": nrm((DEPTH, 6 * D), 0.02),
        "norm_g": 1.0 + nrm((DEPTH, 2, D), 0.02),
        "four_w_out": nrm((nA, D, D), D ** -0.5),
        "diff_w_in": nrm((nB, D, 3 * D), D ** -0.5),
        "diff_lam": nrm((nB, 4, DIFF_HEAD_DIM), 0.1),
        "diff_norm_g": 1.0 + nrm((nB, 2 * DIFF_HEAD_DIM), 0.02),
        "diff_w_out": nrm((nB, D, D), D ** -0.5),
        "ssd_w_in": nrm((nC, D, SSD_IN_DIM), D ** -0.5),
        "ssd_conv_w": nrm((nC, SSD_CONV, SSD_CONV_DIM), SSD_CONV ** -0.5),
        "ssd_conv_b": nrm((nC, SSD_CONV_DIM), 0.02),
        "ssd_a_log": jnp.log(jax.random.uniform(next(ks), (nC, 2, SSD_HEADS), jnp.float32, 1.0, 16.0)),
        "ssd_dt_bias": dt0 + jnp.log(-jnp.expm1(-dt0)),
        "ssd_d": 1.0 + nrm((nC, SSD_HEADS), 0.1),
        "ssd_norm_g": 1.0 + nrm((nC, SSD_D_INNER), 0.02),
        "ssd_w_out": nrm((nC, SSD_D_INNER, D), SSD_D_INNER ** -0.5),
        "hgrn_w_in": nrm((nD, D, 5 * D), D ** -0.5),
        "hgrn_lb": nrm((DEPTH, D), 0.1),
        "hgrn_norm_g": 1.0 + nrm((nD, D), 0.02),
        "hgrn_w_out": nrm((nD, D, D), D ** -0.5),
        "peer_wq": nrm((DEPTH, D, PEER_HEADS * PEER_KEY_DIM), D ** -0.5),
        "peer_keys": nrm((DEPTH, PEER_HEADS, 2, PEER_N_KEYS, PEER_KEY_DIM // 2), (PEER_KEY_DIM // 2) ** -0.5),
        "peer_u": nrm((DEPTH, PEER_EXPERTS, D), D ** -0.5),
        "peer_v": nrm((DEPTH, PEER_EXPERTS, D), 0.25),
        "final_g": 1.0 + nrm((D,), 0.02),
    }

def reference(x, c, ctx, c_ctx, w_mod, b_mod, norm_g, four_w_out, diff_w_in, diff_lam, diff_norm_g,
              diff_w_out, ssd_w_in, ssd_conv_w, ssd_conv_b, ssd_a_log, ssd_dt_bias, ssd_d, ssd_norm_g,
              ssd_w_out, hgrn_w_in, hgrn_lb, hgrn_norm_g, hgrn_w_out, peer_wq, peer_keys, peer_u, peer_v,
              final_g):
    B, L, D = x.shape
    C = ctx.shape[1]
    lower_bounds = jnp.cumsum(jax.nn.softmax(hgrn_lb.astype(jnp.float32), axis=0), axis=0)
    lower_bounds = lower_bounds - lower_bounds[0]
    xl, xc = x, ctx
    for i in range(DEPTH):
        last = i == DEPTH - 1
        kind, j = i % N_MIXERS, i // N_MIXERS
        mod_l = (jax.nn.silu(c) @ w_mod[i] + b_mod[i])[:, None, :]
        mod_c = (jax.nn.silu(c_ctx) @ w_mod[i] + b_mod[i])[None, None, :]
        sh1_l, sc1_l, ga1_l, sh2_l, sc2_l, ga2_l = jnp.split(mod_l, 6, axis=-1)
        sh1_c, sc1_c, ga1_c, sh2_c, sc2_c, ga2_c = jnp.split(mod_c, 6, axis=-1)

        hl = modulate(rmsnorm(xl, norm_g[i, 0]), sh1_l, sc1_l)
        hc = modulate(rmsnorm(xc, norm_g[i, 0]), sh1_c, sc1_c)
        ctx_out = not last
        if kind == 0:
            yc, yl = fourier_mixer(hc, hl, four_w_out[j], ctx_out)
        elif kind == 1:
            yc, yl = diff_attention_mixer(hc, hl, diff_w_in[j], diff_lam[j], diff_norm_g[j],
                                          diff_w_out[j], i, ctx_out)
        elif kind == 2:
            yc, yl = ssd_mixer(hc, hl, ssd_w_in[j], ssd_conv_w[j], ssd_conv_b[j], ssd_a_log[j],
                               ssd_dt_bias[j], ssd_d[j], ssd_norm_g[j], ssd_w_out[j], ctx_out)
        else:
            yc, yl = hgrn2_mixer(hc, hl, hgrn_w_in[j], lower_bounds[i], hgrn_norm_g[j],
                                 hgrn_w_out[j], ctx_out)
        xl = xl + ga1_l * yl
        hl = modulate(rmsnorm(xl, norm_g[i, 1]), sh2_l, sc2_l)
        if last:
            xl = xl + ga2_l * peer_ffn(hl.reshape(B * L, D), peer_wq[i], peer_keys[i],
                                       peer_u[i], peer_v[i]).reshape(B, L, D)
        else:
            xc = xc + ga1_c * yc
            hc = modulate(rmsnorm(xc, norm_g[i, 1]), sh2_c, sc2_c)
            tokens = jnp.concatenate([hl.reshape(B * L, D), hc.reshape(B * C, D)], axis=0)
            out = peer_ffn(tokens, peer_wq[i], peer_keys[i], peer_u[i], peer_v[i])
            xl = xl + ga2_l * out[:B * L].reshape(B, L, D)
            xc = xc + ga2_c * out[B * L:].reshape(B, C, D)
    return rmsnorm(xl, final_g)


_drawn_inputs = setup_inputs


def setup_inputs(seed=0):
    import zlib

    import numpy as np

    out = dict(_drawn_inputs(seed))
    spreads = {}
    factors = {'norm_g': 5.468, 'diff_lam': 2.69, 'diff_norm_g': 24.586, 'final_g': 7.412}
    for name, (base, spread) in spreads.items():
        noise = np.random.default_rng([zlib.crc32(name.encode()), seed]).standard_normal(out[name].shape)
        drawn = base * np.exp(spread * noise) if base else spread * noise
        out[name] = __import__('jax').numpy.asarray(drawn.astype(out[name].dtype))
    for name, factor in factors.items():
        out[name] = (out[name] * factor).astype(out[name].dtype)
    return out
```

```python
import concourse.bass as bass
from concourse import mybir

P = 128
D = 1024
KD = D // P
SEQ, CTX = 512, 256
LT, CT = SEQ // P, CTX // P
NT = LT + CT
GRID_W = 64
GROUPS = 8
HEADS, HEAD_DIM = 8, 64
ROPE_BASE = 10000.0
PEER_HEADS = 8
N_KEYS = 128
EXPERTS = N_KEYS * N_KEYS
TOPK = 16
EPS = 1e-6
LAM_INIT = 0.8 - 0.6 * 0.7408182206817179
SLOTS = 8
BATCH = 2
BATCHES = TOPK // BATCH
AHEAD = SLOTS // BATCH
LOWEST = -3.0e38

X_AT = 0
MOD2_AT = 6144
MOD1_AT = 12288
H_AT = 18432
DFT_L_AT = 24576
DFT_G_AT = 28672
SEL_AT = 30000
RES_AT = 28928
IDENT_AT = 30824
NORM_G_AT = 30952
ROW_AT = 33000
BIAS_AT = 34536
WMOD_AT = 40680
YT_AT = 34536
WOUT_AT = 40680
AB_AT = 48872
DFT_C_AT = 51944
HT_AT = 18432
V_AT = 24576
KT_AT = 30952
QT_AT = 37096
WIN_AT = 41192
ROPE_AT = 49384
ROT_AT = 49896
PROB_AT = 18432
WO_AT = 41192
SUBG_AT = 49384
O_AT = 49896
O2_AT = 12288
OT_AT = 50920
TMP_AT = 51944
HCUR_AT = 12288
HNEXT_AT = 13312
PHT_AT = 14336
DIAG_AT = 15360
QT1_AT = 16384
CAND_AT = 16640
IDX_AT = 17152
PIDENT_AT = 17664
SMALL_AT = 17792
KEYS_AT = 18152
WQ_AT = 20200
RING_AT = 36584
PERS_AT = 52968
ARENA = 53200


def build(nc, x, cc, w_mod, b_mod, norm_g, four_w, diff_w_in, diff_lam, diff_g, diff_w_out, peer_wq,
          keys_t, experts, final_g, dft_l, dft_c, dft_g, rope, ident, iota, out):
    F32, BF16, U32 = mybir.dt.float32, mybir.dt.bfloat16, mybir.dt.uint32
    ALU, ACT, AX = mybir.AluOpType, mybir.ActivationFunctionType, mybir.AxisListType
    ds = bass.ds

    A = nc.alloc_sbuf_tensor("arena", [P, ARENA], F32)
    PS = nc.alloc_psum_tensor("ps", [P, 8 * 512], F32)

    def at(off, *shape):
        n = 1
        for s in shape:
            n *= s
        v = A[:, off:off + n]
        if len(shape) == 2:
            v = v.rearrange("p (a b) -> p a b", b=shape[1])
        if len(shape) == 3:
            v = v.rearrange("p (a b c) -> p a b c", b=shape[1], c=shape[2])
        return v

    def bank(b, n=512):
        return PS[:, b * 512:b * 512 + n]

    X = at(X_AT, NT, D)
    ident_sb = at(IDENT_AT, P)
    pers = at(PERS_AT, 232)
    silu_c = pers[:, 0:16].rearrange("p (k s) -> p k s", s=2)
    c_in = pers[:, 16:32]
    ssq = pers[:, 32:40]
    rstd = pers[:, 40:48]
    lam = pers[:, 48:56]
    eps = pers[:, 56:57]
    neg_max = pers[:, 64:68]
    zsum = pers[:, 72:76]
    rz_at = pers[:, 80:84]
    ossq = pers[:, 88:96]
    orstd = pers[:, 96:104]

    sems = {}

    def sem(name):
        if name not in sems:
            sems[name] = nc.alloc_semaphore(name)
        return sems[name]

    def wait(eng, name, value):
        if not (isinstance(value, int) and value <= 0):
            eng.wait_ge(sem(name), value)

    sel = at(SEL_AT, 2 * P)[0:2, :]

    def modulation(i):
        n = f"m{i}_"
        wm = w_mod[i].rearrange("(k p) n -> p k n", p=P)
        bias = at(BIAS_AT, 6 * D)
        gains = at(NORM_G_AT, 2, D)
        NB = 3
        with nc.Block() as block:
            @block.sync
            def _(sp):
                if i == 0:
                    sp.dma_start(c_in, cc).then_inc(sem("c_in"), 16)
                sp.dma_start(sel, ident_rows).then_inc(sem(n + "tables"), 16)
                sp.dma_start(ident_sb, ident).then_inc(sem(n + "tables"), 16)
                sp.dma_start(bias[0:2, :], b_mod[i:i + 1, :].to_broadcast([2, 6 * D])).then_inc(sem(n + "bias"), 16)
                sp.dma_start(gains, norm_g[i:i + 1, :, :].to_broadcast([P, 2, D])).then_inc(sem(n + "gains"), 16)
                for ch in range(12):
                    wait(sp, n + "product", ch - NB + 1)
                    sp.dma_start(at(WMOD_AT + 4096 * (ch % NB), KD, 512), wm[:, :, ch * 512:(ch + 1) * 512]
                                 ).then_inc(sem(n + f"w{ch % NB}"), 16)
                    if i == 0 and ch == 3:
                        sp.dma_start(X, x.rearrange("(t p) d -> p t d", p=P)).then_inc(sem("x_in"), 16)
                    if i == 0 and ch == 5:
                        sp.dma_start(at(DFT_L_AT, 4096), dft_l).then_inc(sem("dft_in"), 16)
                        sp.dma_start(at(DFT_G_AT, 256), dft_g).then_inc(sem("dft_in"), 16)

            @block.tensor
            def _(pe):
                pe.wait_ge(sem("silu"), 1)
                pe.wait_ge(sem(n + "tables"), 32)

                def spread_rows(ch):
                    pe.wait_ge(sem(n + "row"), ch + 1)
                    wait(pe, n + "spread_out", ch - 1)
                    for s in range(2):
                        last = nc.tensor.matmul(bank(2 + 2 * (ch % 2) + s), sel[:, s * P:(s + 1) * P],
                                                at(ROW_AT + 512 * (ch % NB), 512)[0:2, :], start=True, stop=True)
                    last.then_inc(sem(n + "spread"), 1)

                for ch in range(12):
                    pe.wait_ge(sem(n + f"w{ch % NB}"), 16 * (ch // NB + 1))
                    wait(pe, n + "row", ch - 1)
                    w = at(WMOD_AT + 4096 * (ch % NB), KD, 512)
                    for k in range(KD):
                        last = nc.tensor.matmul(bank(ch % 2)[0:2, :], silu_c[:, k, :], w[:, k, :],
                                                start=(k == 0), stop=(k == KD - 1))
                    last.then_inc(sem(n + "product"), 1)
                    if ch >= 1:
                        spread_rows(ch - 1)
                spread_rows(11)

            @block.vector
            def _(dve):
                dve.wait_ge(sem(n + "bias"), 16)
                for ch in range(12):
                    dve.wait_ge(sem(n + "product"), ch + 1)
                    wait(dve, n + "spread", ch - NB + 1)
                    nc.vector.tensor_tensor(at(ROW_AT + 512 * (ch % NB), 512)[0:2, :], bank(ch % 2)[0:2, :],
                                            bias[0:2, ch * 512:(ch + 1) * 512], ALU.add
                                            ).then_inc(sem(n + "row"), 1)

            @block.scalar
            def _(act):
                if i == 0:
                    act.wait_ge(sem("c_in"), 16)
                    nc.scalar.activation(silu_c.rearrange("p k s -> p (k s)"), c_in, ACT.Silu
                                         ).then_inc(sem("silu"), 1)
                for ch in range(12):
                    kind, half = ch // 2, ch % 2
                    base = (MOD1_AT if kind < 3 else MOD2_AT) + (kind % 3) * 2 * D
                    act.wait_ge(sem(n + "spread"), ch + 1)
                    for s in range(2):
                        last = nc.scalar.copy(at(base + s * D + half * 512, 512), bank(2 + 2 * (ch % 2) + s))
                    last.then_inc(sem(n + "spread_out"), 1)

            @block.gpsimd
            def _(pool):
                pool.wait_ge(sem(n + "gains"), 16)
                for norm, base in enumerate((MOD1_AT, MOD2_AT)):
                    pool.wait_ge(sem(n + "spread_out"), 6 * norm + 4)
                    for s in range(2):
                        v = at(base + 2 * D + s * D, D)
                        nc.gpsimd.tensor_scalar_add(v, v, 1.0).then_inc(sem(n + "plus_one"), 1)
                        pool.wait_ge(sem(n + "plus_one"), 2 * norm + s + 1)
                        nc.gpsimd.tensor_tensor(v, v, gains[:, norm, :], ALU.mult)

    ident_rows = rope[1]
    rope_t = rope[0]

    def mod_row(base, kind, stream):
        return at(base + kind * 2 * D + stream * D, D)

    def square_sums(tiles, junk, signal):
        for t in range(tiles):
            nc.scalar.activation(junk, X[:, t, :], ACT.Square, accum_out=ssq[:, t:t + 1])
            nc.scalar.drain()
        nc.scalar.activation(rstd[:, 0:tiles], ssq[:, 0:tiles], ACT.Sqrt, scale=1.0 / D, bias=eps
                             ).then_inc(sem(signal), 1)

    def fourier_layer():
        H = at(H_AT, NT, D)
        dftL = at(DFT_L_AT, 2, LT, 512)
        dftC = at(DFT_C_AT, 2, CT, 256)
        dftG = at(DFT_G_AT, 2, P)
        wout = at(WOUT_AT, KD, D)
        YT = at(YT_AT, GROUPS, SEQ + CTX)
        res = at(RES_AT, D)

        def chan_out(act, g):
            act.wait_ge(sem("f_chan"), g + 1)
            nc.scalar.copy(YT[:, g, 0:SEQ], bank(3))
            nc.scalar.copy(YT[:, g, SEQ:], bank(4, 256)).then_inc(sem("f_chan_out"), 1)

        with nc.Block() as block:
            @block.sync
            def _(sp):
                sp.dma_start(at(DFT_C_AT, 1024), dft_c).then_inc(sem("dftc_in"), 16)
                sp.dma_start(wout, four_w.rearrange("(k p) n -> p k n", p=P)).then_inc(sem("wout_in"), 16)

            @block.scalar
            def _(act):
                act.wait_ge(sem("x_in"), 16)
                act.wait_ge(sem("eps"), 1)
                square_sums(NT, at(TMP_AT - 2048, D), "f_rms")
                for g in range(GROUPS):
                    act.wait_ge(sem("f_token"), g + 1)
                    wait(act, "f_chan", g - 1)
                    ab = at(AB_AT + 1536 * (g % 2), 2, 768)
                    nc.scalar.copy(ab[:, 1, 0:SEQ], bank(1))
                    nc.scalar.copy(ab[:, 1, SEQ:], bank(7, 256)).then_inc(sem("f_sin"), 1)
                    if g >= 1:
                        chan_out(act, g - 1)
                chan_out(act, GROUPS - 1)

            @block.vector
            def _(dve):
                nc.vector.memset(eps, EPS).then_inc(sem("eps"), 1)
                dve.wait_ge(sem("f_rms"), 1)
                nc.vector.reciprocal(rstd[:, 0:NT], rstd[:, 0:NT])
                dve.drain()
                for t in range(NT):
                    s = t // LT
                    nc.vector.scalar_tensor_tensor(out=H[:, t, :], in0=X[:, t, :], scalar=rstd[:, t:t + 1],
                                                   in1=mod_row(MOD1_AT, 1, s), op0=ALU.mult, op1=ALU.mult)
                    dve.drain()
                    nc.vector.tensor_tensor(H[:, t, :], H[:, t, :], mod_row(MOD1_AT, 0, s), ALU.add
                                            ).then_inc(sem("f_norm"), 1)
                for g in range(GROUPS):
                    dve.wait_ge(sem("f_token"), g + 1)
                    wait(dve, "f_chan", g - 1)
                    ab = at(AB_AT + 1536 * (g % 2), 2, 768)
                    nc.vector.tensor_copy(ab[:, 0, 0:SEQ], bank(0))
                    nc.vector.tensor_copy(ab[:, 0, SEQ:], bank(2, 256)).then_inc(sem("f_cos"), 1)
                for t in range(NT):
                    dve.wait_ge(sem("f_out"), t + 1)
                    nc.vector.tensor_tensor(res, PS[:, 512 * (5 if t % 2 else 0):][:, 0:D],
                                            mod_row(MOD1_AT, 2, t // LT), ALU.mult).then_inc(sem("f_out_read"), 1)
                    dve.drain()
                    nc.vector.tensor_tensor(X[:, t, :], X[:, t, :], res, ALU.add)
                    dve.drain()

            @block.tensor
            def _(pe):
                def token_transform(g):
                    wait(pe, "f_cos", g)
                    wait(pe, "f_sin", g)
                    for tab in range(2):
                        for k in range(LT):
                            nc.tensor.matmul(bank(tab), H[:, k, g * P:(g + 1) * P], dftL[:, tab, k, :],
                                             start=(k == 0), stop=(k == LT - 1))
                    for tab in range(2):
                        for k in range(CT):
                            last = nc.tensor.matmul(bank(7 if tab else 2, 256),
                                                    H[:, LT + k, g * P:(g + 1) * P], dftC[:, tab, k, :],
                                                    start=(k == 0), stop=(k == CT - 1))
                    last.then_inc(sem("f_token"), 1)

                def channel_transform(g):
                    pe.wait_ge(sem("f_cos"), g + 1)
                    pe.wait_ge(sem("f_sin"), g + 1)
                    wait(pe, "f_chan_out", g)
                    ab = at(AB_AT + 1536 * (g % 2), 2, 768)
                    for o, lo, hi in ((bank(3), 0, SEQ), (bank(4, 256), SEQ, SEQ + CTX)):
                        for tab in range(2):
                            last = nc.tensor.matmul(o, dftG[:, tab, :], ab[:, tab, lo:hi],
                                                    start=(tab == 0), stop=(tab == 1))
                    last.then_inc(sem("f_chan"), 1)

                pe.wait_ge(sem("f_norm"), NT)
                pe.wait_ge(sem("dft_in"), 32)
                pe.wait_ge(sem("dftc_in"), 16)
                for g in range(GROUPS):
                    token_transform(g)
                    if g >= 1:
                        channel_transform(g - 1)
                channel_transform(GROUPS - 1)
                pe.wait_ge(sem("wout_in"), 16)
                pe.wait_ge(sem("f_chan_out"), GROUPS)
                for t in range(NT):
                    wait(pe, "f_out_read", t - 1)
                    b = 5 if t % 2 else 0
                    for half in range(2):
                        for k in range(KD):
                            last = nc.tensor.matmul(bank(b + half), YT[:, k, t * P:(t + 1) * P],
                                                    wout[:, k, half * 512:(half + 1) * 512],
                                                    start=(k == 0), stop=(k == KD - 1))
                    last.then_inc(sem("f_out"), 1)

    def attention_layer():
        HT = at(HT_AT, NT, KD, P)
        V = at(V_AT, NT, D)
        KT = at(KT_AT, HEADS, SEQ + CTX)
        QT = at(QT_AT, HEADS, SEQ)
        htmp = at(V_AT, 2, D)
        rope_sb = at(ROPE_AT, LT, 2, 64)
        w_in = diff_w_in.rearrange("(k p) n -> p k n", p=P)
        QCH = [(0, LT), (1, LT), (2, NT), (3, NT), (4, NT), (5, NT)]
        STEPS = [(c, t) for c, n in QCH for t in range(n)]

        with nc.Block() as block:
            @block.sync
            def _(sp):
                sp.dma_start(at(ROPE_AT, LT * 128), rope_t).then_inc(sem("rope_in"), 16)
                for c in range(2):
                    sp.dma_start(at(WIN_AT + 4096 * c, KD, 512), w_in[:, :, c * 512:(c + 1) * 512]
                                 ).then_inc(sem(f"win{c}"), 16)

            @block.scalar
            def _(act):
                square_sums(NT, at(TMP_AT, D), "a_rms")
                for t in range(NT):
                    act.wait_ge(sem("a_tr"), t + 1)
                    nc.scalar.copy(at(HT_AT + t * D, D), PS[:, (t % 2) * D:(t % 2 + 1) * D]
                                   ).then_inc(sem("a_tr_out"), 1)

            @block.vector
            def _(dve):
                dve.wait_ge(sem("a_rms"), 1)
                nc.vector.reciprocal(rstd[:, 0:NT], rstd[:, 0:NT])
                dve.drain()
                for t in range(NT):
                    s = t // LT
                    wait(dve, "a_tr", t - 1)
                    nc.vector.scalar_tensor_tensor(out=htmp[:, t % 2, :], in0=X[:, t, :], scalar=rstd[:, t:t + 1],
                                                   in1=mod_row(MOD1_AT, 1, s), op0=ALU.mult, op1=ALU.mult)
                    dve.drain()
                    nc.vector.tensor_tensor(htmp[:, t % 2, :], htmp[:, t % 2, :], mod_row(MOD1_AT, 0, s), ALU.add
                                            ).then_inc(sem("a_norm"), 1)

            @block.tensor
            def _(pe):
                for t in range(NT):
                    pe.wait_ge(sem("a_norm"), t + 1)
                    wait(pe, "a_tr_out", t - 1)
                    for k in range(KD):
                        last = nc.tensor.transpose(PS[:, (t % 2) * D + k * P:(t % 2) * D + (k + 1) * P],
                                                   htmp[:, t % 2, k * P:(k + 1) * P], ident_sb)
                    last.then_inc(sem("a_tr"), 1)

        with nc.Block() as block:
            @block.sync
            def _(sp):
                done = 0
                for c, n in QCH:
                    if c >= 2:
                        sp.wait_ge(sem("p_mm"), done)
                        sp.dma_start(at(WIN_AT + 4096 * (c % 2), KD, 512), w_in[:, :, c * 512:(c + 1) * 512]
                                     ).then_inc(sem(f"win{c % 2}"), 16)
                        done += QCH[c - 1][1]
                    else:
                        done = QCH[0][1]

            @block.tensor
            def _(pe):
                def turn(i):
                    j = i
                    pe.wait_ge(sem("p_rot"), j + 1)
                    wait(pe, "p_turn_out", j - 1)
                    for q in range(4):
                        last = nc.tensor.transpose(bank(2 + j % 2)[:, q * P:(q + 1) * P],
                                                   at(ROT_AT + 512 * (j % 2), 512)[:, q * P:(q + 1) * P], ident_sb)
                    last.then_inc(sem("p_turn"), 1)

                for i, (c, t) in enumerate(STEPS):
                    pe.wait_ge(sem(f"win{c % 2}"), 16 * (c // 2 + 1))
                    wait(pe, "p_read", i - 1)
                    w = at(WIN_AT + 4096 * (c % 2), KD, 512)
                    for k in range(KD):
                        last = nc.tensor.matmul(bank(i % 2), HT[:, t, k, :], w[:, k, :],
                                                start=(k == 0), stop=(k == KD - 1))
                    last.then_inc(sem("p_mm"), 1)
                    if i >= 1 and STEPS[i - 1][0] < 4:
                        turn(i - 1)

            @block.vector
            def _(dve):
                dve.wait_ge(sem("rope_in"), 16)
                for i, (c, t) in enumerate(STEPS):
                    dve.wait_ge(sem("p_mm"), i + 1)
                    src = bank(i % 2)
                    if c >= 4:
                        nc.vector.tensor_copy(V[:, t, (c - 4) * 512:(c - 3) * 512], src).then_inc(sem("p_read"), 1)
                        continue
                    wait(dve, "p_turn", i - 1)
                    rot = at(ROT_AT + 512 * (i % 2), 512)
                    if t >= LT:
                        nc.vector.tensor_copy(rot, src).then_inc(sem("p_read"), 1)
                        nc.vector.drain().then_inc(sem("p_rot"), 1)
                        continue
                    cos = rope_sb[:, t, 0:1, :].to_broadcast([P, 8, 64])
                    nc.vector.tensor_tensor(rot.rearrange("p (h d) -> p h d", d=64),
                                            src.rearrange("p (h d) -> p h d", d=64), cos, ALU.mult)
                    tmp = at(TMP_AT, 512)
                    t4 = tmp.rearrange("p (h a b f) -> p h a b f", a=2, b=2, f=16)
                    s4 = src.rearrange("p (h a b f) -> p h a b f", a=2, b=2, f=16)
                    sin = rope_sb[:, t, 1, :].rearrange("p (a b f) -> p a b f", a=2, b=2)
                    for a in range(2):
                        for b in range(2):
                            sb_ = sin[:, a, b, :].unsqueeze(1).to_broadcast([P, 8, 16])
                            last = nc.vector.tensor_tensor(t4[:, :, a, b, :], s4[:, :, a, 1 - b, :], sb_, ALU.mult)
                    last.then_inc(sem("p_read"), 1)
                    dve.drain()
                    nc.vector.tensor_tensor(rot, rot, tmp, ALU.add).then_inc(sem("p_rot"), 1)
                    dve.drain()

            @block.scalar
            def _(act):
                for i, (c, t) in enumerate(STEPS):
                    if c >= 4:
                        break
                    act.wait_ge(sem("p_turn"), i + 1)
                    dst, h0 = (QT, 4 * c) if c < 2 else (KT, 4 * (c - 2))
                    nc.scalar.copy(dst[:, h0:h0 + 4, t * P:(t + 1) * P],
                                   bank(2 + i % 2).rearrange("p (q n) -> p q n", n=P)).then_inc(sem("p_turn_out"), 1)

        scale = float(HEAD_DIM) ** -0.5
        K = SEQ + CTX
        wo = at(WO_AT, KD, D)
        OT = at(OT_AT, KD, P)
        tmp = at(TMP_AT, D)
        subg = at(SUBG_AT, P)
        lam_in = at(SUBG_AT + P, 256)
        UNITS = [(m, h) for m in range(LT) for h in range(HEADS)]

        turn_ps = PS[:, 6 * 512:6 * 512 + K]
        o_ps = PS[:, 6 * 512 + K:6 * 512 + K + P]

        def prob(i):
            return at(PROB_AT + 4 * K * (i % 2), 4, K)

        def score_ps(i):
            return PS[:, 3 * 512 * (i % 2):3 * 512 * (i % 2 + 1)]

        def O(m):
            return at(O_AT if m % 2 == 0 else O2_AT, HEADS, P)

        with nc.Block() as block:
            @block.sync
            def _(sp):
                sp.dma_start(lam_in, diff_lam.to_broadcast([P, 256])).then_inc(sem("lam_in"), 16)
                sp.dma_start(subg, diff_g.to_broadcast([P, P])).then_inc(sem("lam_in"), 16)
                sp.dma_start(wo, diff_w_out.rearrange("(k p) n -> p k n", p=P)).then_inc(sem("wo_in"), 16)

            @block.tensor
            def _(pe):
                def scores(i):
                    m, h = UNITS[i]
                    wait(pe, "t_exp", i - 1)
                    for c, lo, hi in ((0, 512, K), (0, 0, 512), (1, 1024 - K, K), (1, 0, 1024 - K)):
                        if (c, lo) == (1, 0):
                            pe.wait_ge(sem("t_shared"), i + 1)
                        last = nc.tensor.matmul(score_ps(i)[:, c * K + lo:c * K + hi],
                                                QT[64 * c:64 * c + 64, h, m * P:(m + 1) * P],
                                                KT[64 * c:64 * c + 64, h, lo:hi], start=True, stop=True)
                        if (c, lo) == (0, 512):
                            last.then_inc(sem("t_shared"), 1)
                    last.then_inc(sem("t_scores"), 1)

                def turn(i):
                    pe.wait_ge(sem("t_diff"), i + 1)
                    wait(pe, "t_o_out", i)
                    for k in range(NT):
                        last = nc.tensor.transpose(turn_ps[:, k * P:(k + 1) * P],
                                                   prob(i)[:, 2, k * P:(k + 1) * P], ident_sb)
                    last.then_inc(sem("t_turn"), 1)

                def mix(i):
                    m, h = UNITS[i]
                    aT = prob(i)[:, 3, :]
                    pe.wait_ge(sem("t_turn_out"), i + 1)
                    for k in range(NT):
                        last = nc.tensor.matmul(o_ps, aT[:, k * P:(k + 1) * P], V[:, k, h * P:(h + 1) * P],
                                                start=(k == 0), stop=(k == NT - 1))
                    last.then_inc(sem("t_o"), 1)

                def project(m):
                    pe.wait_ge(sem("t_onorm"), m + 1)
                    pe.wait_ge(sem("t_o_out"), HEADS * (m + 1) + (2 if m < LT - 1 else 0))
                    for half in range(2):
                        for k in range(4):
                            last = nc.tensor.transpose(bank(6 + half)[:, k * P:(k + 1) * P], O(m)[:, 4 * half + k, :],
                                                       ident_sb)
                    last.then_inc(sem("t_oT"), 1)
                    pe.wait_ge(sem("t_oT_out"), m + 1)
                    for half in range(2):
                        for k in range(KD):
                            last = nc.tensor.matmul(bank(6 + half), OT[:, k, :], wo[:, k, half * 512:(half + 1) * 512],
                                                    start=(k == 0), stop=(k == KD - 1))
                    last.then_inc(sem("t_y"), 1)
                    pe.wait_ge(sem("t_y_out"), m + 1)

                scores(0)
                scores(1)
                pe.wait_ge(sem("wo_in"), 16)
                for i, (m, h) in enumerate(UNITS):
                    turn(i)
                    if i + 2 < len(UNITS):
                        scores(i + 2)
                    mix(i)
                    if h == 1 and m > 0:
                        project(m - 1)
                project(LT - 1)

            @block.scalar
            def _(act):
                def exponentials(i):
                    act.wait_ge(sem("t_max"), i + 1)
                    wait(act, "t_diff", i - 1)
                    for c in range(2):
                        last = nc.scalar.activation(prob(i)[:, c, :], score_ps(i)[:, c * K:(c + 1) * K], ACT.Exp,
                                                    scale=scale,
                                                    bias=neg_max[:, 2 * (i % 2) + c:2 * (i % 2) + c + 1],
                                                    accum_out=zsum[:, 2 * (i % 2) + c:2 * (i % 2) + c + 1])
                    act.drain().then_inc(sem("t_exp"), 1)

                def tile_turn(m):
                    act.wait_ge(sem("t_oT"), m + 1)
                    nc.scalar.copy(at(OT_AT, D), PS[:, 6 * 512:8 * 512]).then_inc(sem("t_oT_out"), 1)

                def tile_rms(m):
                    act.wait_ge(sem("t_ossq"), m + 1)
                    nc.scalar.activation(orstd, ossq, ACT.Sqrt, scale=1.0 / P, bias=eps).then_inc(sem("t_orms"), 1)

                act.wait_ge(sem("t_lam_sum"), 1)
                nc.scalar.activation(lam[:, 2:4], lam[:, 0:2], ACT.Exp).then_inc(sem("t_lam_exp"), 1)
                exponentials(0)
                for i, (m, h) in enumerate(UNITS):
                    if i + 1 < len(UNITS):
                        exponentials(i + 1)
                    act.wait_ge(sem("t_turn"), i + 1)
                    wait(act, "t_o", i - 1)
                    nc.scalar.copy(prob(i)[:, 3, :], turn_ps).then_inc(sem("t_turn_out"), 1)
                    if h == 0 and m > 0:
                        tile_rms(m - 1)
                    if h == 1 and m > 0:
                        tile_turn(m - 1)
                tile_rms(LT - 1)
                tile_turn(LT - 1)

            @block.vector
            def _(dve):
                dve.wait_ge(sem("lam_in"), 32)
                for j in range(2):
                    nc.vector.tensor_tensor_reduce(out=tmp[:, 0:64], in0=lam_in[:, 128 * j:128 * j + 64],
                                                   in1=lam_in[:, 128 * j + 64:128 * j + 128], scale=1.0, scalar=0.0,
                                                   op0=ALU.mult, op1=ALU.add, accum_out=lam[:, j:j + 1])
                    dve.drain()
                nc.vector.tensor_scalar(subg, subg, 1.0 - LAM_INIT, None, ALU.mult).then_inc(sem("t_lam_sum"), 1)
                dve.wait_ge(sem("t_lam_exp"), 1)
                nc.vector.tensor_tensor(lam[:, 4:5], lam[:, 2:3], lam[:, 3:4], ALU.subtract)
                dve.drain()
                nc.vector.tensor_scalar(lam[:, 5:6], lam[:, 4:5], LAM_INIT, None, ALU.add)
                dve.drain()

                def maxima(i):
                    dve.wait_ge(sem("t_scores"), i + 1)
                    nm = neg_max[:, 2 * (i % 2):2 * (i % 2) + 2]
                    nc.vector.reduce_max(nm, score_ps(i).rearrange("p (c n) -> p c n", c=2), AX.X)
                    dve.drain()
                    nc.vector.tensor_scalar(nm, nm, -scale, None, ALU.mult).then_inc(sem("t_max"), 1)

                def difference(i):
                    pr, z, r = prob(i), zsum[:, 2 * (i % 2):2 * (i % 2) + 2], rz_at[:, 2 * (i % 2):2 * (i % 2) + 2]
                    dve.wait_ge(sem("t_exp"), i + 1)
                    wait(dve, "t_turn", i - 1)
                    nc.vector.reciprocal(r, z)
                    dve.drain()
                    nc.vector.tensor_scalar(pr[:, 1, :], pr[:, 1, :], r[:, 1:2], lam[:, 5:6], ALU.mult, ALU.mult)
                    dve.drain()
                    nc.vector.scalar_tensor_tensor(out=pr[:, 2, :], in0=pr[:, 0, :], scalar=r[:, 0:1], in1=pr[:, 1, :],
                                                   op0=ALU.mult, op1=ALU.subtract).then_inc(sem("t_diff"), 1)

                def head_out(i):
                    m, h = UNITS[i]
                    dve.wait_ge(sem("t_o"), i + 1)
                    if h == 0:
                        wait(dve, "t_oT", m - 1)
                    nc.vector.tensor_copy(O(m)[:, h, :], o_ps).then_inc(sem("t_o_out"), 1)

                def tile_norm(m):
                    o = O(m)
                    dve.drain()
                    sq = tmp.rearrange("p (h n) -> p h n", n=P)
                    nc.vector.tensor_tensor(sq, o, o, ALU.mult)
                    dve.drain()
                    nc.vector.reduce_sum(ossq, sq, AX.X).then_inc(sem("t_ossq"), 1)
                    nc.vector.tensor_tensor(o, o, subg.unsqueeze(1).to_broadcast([P, HEADS, P]), ALU.mult)
                    dve.wait_ge(sem("t_orms"), m + 1)
                    dve.drain()
                    nc.vector.reciprocal(orstd, orstd)
                    dve.drain()
                    nc.vector.tensor_tensor(o, o, orstd.unsqueeze(2).to_broadcast([P, HEADS, P]), ALU.mult
                                            ).then_inc(sem("t_onorm"), 1)

                def tile_out(m):
                    dve.wait_ge(sem("t_y"), m + 1)
                    nc.vector.tensor_tensor(tmp, PS[:, 6 * 512:8 * 512], mod_row(MOD1_AT, 2, 0), ALU.mult
                                            ).then_inc(sem("t_y_out"), 1)
                    dve.drain()
                    nc.vector.tensor_tensor(X[:, m, :], X[:, m, :], tmp, ALU.add)
                    dve.drain()

                maxima(0)
                for i, (m, h) in enumerate(UNITS):
                    if i + 1 < len(UNITS):
                        maxima(i + 1)
                    difference(i)
                    if i >= 1:
                        head_out(i - 1)
                    if h == 0 and m > 0:
                        tile_norm(m - 1)
                    if h == 2 and m > 0:
                        tile_out(m - 1)
                head_out(len(UNITS) - 1)
                tile_norm(LT - 1)
                tile_out(LT - 1)

    def peer(layer, tiles):
        n_ = f"e{layer}_"
        S = lambda name: sem(n_ + name)
        W = lambda eng, name, value: wait(eng, n_ + name, value)

        def wait_apart(eng, name, value):
            W(eng, name, value)
            if not isinstance(value, int):
                eng.sem_inc(S(name + "_seen"), 1)

        hcur, hnext = at(HCUR_AT, D), at(HNEXT_AT, D)
        hT = at(PHT_AT, KD, P)
        diag = at(DIAG_AT, SLOTS, P)
        q_sb, qT = at(CAND_AT, 256), at(QT1_AT, 2, P)
        cand, masked = at(CAND_AT, 256), at(CAND_AT + 256, 256)
        grid2 = at(CAND_AT, 512)
        pid = at(PIDENT_AT, P)
        keys = at(KEYS_AT, 2 * PEER_HEADS * N_KEYS)
        wq = at(WQ_AT, KD * 2048)
        ring = at(RING_AT, SLOTS, 2 * D)
        small = at(SMALL_AT, 360)
        top = small[:, 0:32]
        top_i = small[:, 32:64].bitcast(U32)
        best = small[:, 64:80]
        pos = small[:, 80:112].bitcast(U32)
        rank = small[:, 112:144]
        top_f = small[:, 144:176]
        part = small[:, 176:208]
        shifted = small[:, 208:224]
        expo = small[:, 224:240]
        total = small[:, 240:241]
        rtotal = small[:, 241:242]
        gate_next = small[:, 244:260]
        gate = small[:, 260:276]
        idx_f = small[:, 276:292]
        idx2 = at(IDX_AT, 2 * TOPK).bitcast(U32)
        dots = small[:, 308:324]
        act_out = small[:, 324:340]
        iota_sb = small[:, 340:356]
        r1 = small[:, 356:357]
        s1 = small[:, 357:358]
        zero = small[:, 358:359]
        acc, q_ps, qT_ps, s_ps = PS[:, 0:D], bank(2, 256), bank(3, 256), bank(4, 256)
        hT_ps = PS[:, 5 * 512:5 * 512 + D]

        def q_product(pe, r, head):
            W(pe, "wq", head * 16 + 16)
            for k in range(KD):
                last = nc.tensor.matmul(q_ps, hT[:, k, :], wq[:, ds(head * 256 + k * 2048, 256)],
                                        start=(k == 0), stop=(k == KD - 1))
            last.then_inc(S("q"), 1)

        def q_turn(pe, r):
            W(pe, "q_out", r + 1)
            for c in range(2):
                last = nc.tensor.transpose(qT_ps[:, c * P:(c + 1) * P], q_sb[:, c * P:(c + 1) * P], pid)
            last.then_inc(S("qT"), 1)

        def key_product(pe, r, head):
            W(pe, "qT_out", r + 1)
            for c in range(2):
                last = nc.tensor.matmul(s_ps[:, c * P:(c + 1) * P], qT[:, c, :],
                                        keys[:, ds(head * 256 + c * P, P)], start=True, stop=True)
            last.then_inc(S("scores"), 1)

        def copy_q(act, r):
            W(act, "q", r + 1)
            W(act, "idx", r)
            nc.scalar.copy(q_sb, q_ps).then_inc(S("q_out"), 1)

        def copy_qT(act, r):
            W(act, "qT", r + 1)
            W(act, "scores", r)
            nc.scalar.copy(at(QT1_AT, 256), qT_ps).then_inc(S("qT_out"), 1)

        def gate_exp(act, r):
            W(act, "best", r + 1)
            nc.scalar.activation(expo, shifted, ACT.Exp, accum_out=total)
            act.drain().then_inc(S("expo"), 1)

        def top_keys(dve, r):
            wait_apart(dve, "scores", r + 1)
            for o in (0, 8):
                src = [s_ps[:, 0:P], s_ps[:, P:2 * P]] if o == 0 else [masked[:, 0:P], masked[:, P:2 * P]]
                for c in range(2):
                    nc.vector.max(top[:, 16 * c + o:16 * c + o + 8], src[c])
                dve.drain()
                for c in range(2):
                    nc.vector.max_index(top_i[:, 16 * c + o:16 * c + o + 8], top[:, 16 * c + o:16 * c + o + 8], src[c])
                    if o == 0:
                        nc.vector.match_replace(masked[:, c * P:(c + 1) * P], top[:, 16 * c:16 * c + 8], src[c], LOWEST)
                dve.drain()

        def top_pairs(dve, r):
            nc.vector.tensor_tensor(cand.rearrange("p (a b) -> p a b", b=TOPK),
                                    top[:, 0:16].unsqueeze(2).to_broadcast([P, TOPK, TOPK]),
                                    top[:, 16:32].unsqueeze(1).to_broadcast([P, TOPK, TOPK]), ALU.add)
            nc.vector.tensor_copy(top_f, top_i)
            dve.drain()
            nc.vector.max(best[:, 0:8], cand)
            dve.drain()
            nc.vector.max_index(pos[:, 0:8], best[:, 0:8], cand)
            nc.vector.match_replace(masked, best[:, 0:8], cand, LOWEST)
            dve.drain()
            nc.vector.max(best[:, 8:16], masked)
            dve.drain()
            nc.vector.max_index(pos[:, 8:16], best[:, 8:16], masked)
            nc.vector.tensor_scalar(shifted, best, best[:, 0:1], None, ALU.subtract).then_inc(S("best"), 1)
            dve.drain()

        def expert_numbers(dve, r):
            nc.vector.tensor_scalar(pos[:, 16:32], pos[:, 0:16], 15, None, ALU.bitwise_and)
            dve.drain()
            nc.vector.tensor_scalar(pos[:, 0:16], pos[:, 0:16], 4, None, ALU.logical_shift_right)
            dve.drain()
            nc.vector.tensor_copy(rank, pos)
            dve.drain()
            g3 = grid2.rearrange("p (a b) -> p a b", b=TOPK)
            nc.vector.tensor_tensor(g3, rank.unsqueeze(2).to_broadcast([P, 32, TOPK]),
                                    iota_sb.unsqueeze(1).to_broadcast([P, 32, TOPK]), ALU.is_equal)
            dve.drain()
            for c in range(2):
                nc.vector.tensor_tensor(g3[:, 16 * c:16 * c + 16, :], g3[:, 16 * c:16 * c + 16, :],
                                        top_f[:, 16 * c:16 * c + 16].unsqueeze(1).to_broadcast([P, TOPK, TOPK]),
                                        ALU.mult)
            dve.drain()
            nc.vector.reduce_sum(part, g3, AX.X)
            dve.drain()
            W(dve, "idx_taken", r)
            nc.vector.scalar_tensor_tensor(out=idx_f, in0=part[:, 0:16], scalar=float(N_KEYS), in1=part[:, 16:32],
                                           op0=ALU.mult, op1=ALU.add).then_inc(S("idx"), 1)

        def gates(dve, r):
            W(dve, "expo", r + 1)
            nc.vector.reciprocal(rtotal, total)
            dve.drain()
            nc.vector.tensor_scalar(gate_next, expo, rtotal, None, ALU.mult)

        def pe_unit(pe, u, next_head, route, first=None):
            if route:
                if first is not None:
                    turn_h(pe, first)
                    W(pe, "hT_out", first + 1)
                q_product(pe, u + 1, next_head)
            for b in range(BATCHES):
                W(pe, "diag", u * BATCHES + b + 1)
                for j in range(BATCH):
                    s = (b * BATCH + j) % SLOTS
                    for half in range(2):
                        last = nc.tensor.matmul(acc[:, half * 512:(half + 1) * 512], diag[:, s, :],
                                                ring[:, s, D + half * 512:D + (half + 1) * 512],
                                                start=False, stop=False, skip_group_check=True)
                last.then_inc(S("slots_free"), 1)
                if route and b == 0:
                    q_turn(pe, u + 1)
                if route and b == 1:
                    key_product(pe, u + 1, next_head)

        def act_unit(act, u, route, first=None):
            if route and first is not None:
                copy_h(act, first)
            for b in range(BATCHES):
                W(act, "dots", u * BATCHES + b + 1)
                nc.scalar.activation(act_out[:, b * BATCH:(b + 1) * BATCH], dots[:, b * BATCH:(b + 1) * BATCH],
                                     ACT.Gelu).then_inc(S("gelu"), 1)
                if route and b == 0:
                    copy_q(act, u + 1)
                if route and b == 1:
                    copy_qT(act, u + 1)
                if route and b == 4:
                    gate_exp(act, u + 1)

        def dve_unit(dve, u, route):
            def diagonals(b):
                W(dve, "gelu", u * BATCHES + b + 1)
                for j in range(b * BATCH, (b + 1) * BATCH):
                    last = nc.vector.tensor_scalar(diag[:, j % SLOTS, :], pid, act_out[:, j:j + 1], gate[:, j:j + 1],
                                                   ALU.mult, ALU.mult)
                last.then_inc(S("diag"), 1)

            dve.drain()
            nc.vector.tensor_copy(gate, gate_next)
            dve.drain()
            for b in range(BATCHES):
                for j in range(b * BATCH, (b + 1) * BATCH):
                    W(dve, f"landed{j % SLOTS}", u * 32 + 16 * (j // SLOTS + 1))
                    last = nc.vector.tensor_tensor_reduce(out=ring[:, j % SLOTS, 0:D], in0=ring[:, j % SLOTS, 0:D], in1=hcur, scale=1.0,
                                                          scalar=0.0, op0=ALU.mult, op1=ALU.add,
                                                          accum_out=dots[:, j:j + 1])
                last.then_inc(S("dots"), 1)
                if b >= 1:
                    diagonals(b - 1)
                if route and b == 3:
                    top_keys(dve, u + 1)
                    top_pairs(dve, u + 1)
                if route and b == 4:
                    expert_numbers(dve, u + 1)
                if route and b == 5:
                    gates(dve, u + 1)
            diagonals(BATCHES - 1)

        def pool_unit(pool, u, parity):
            idx = idx2[:, parity * TOPK:(parity + 1) * TOPK]
            wait_apart(pool, "idx", u + 1)
            nc.gpsimd.tensor_scalar_add(idx, idx_f, float(layer * EXPERTS)).then_inc(S("idx_taken"), 1)
            wait_apart(pool, "idx_taken", u + 1)
            for b in range(BATCHES):
                wait_apart(pool, "slots_free", u * BATCHES + b + 1)
                for j in range(b * BATCH, (b + 1) * BATCH):
                    nc.gpsimd.indirect_dma_start(out=ring[:, j % SLOTS, :], out_offset=None, in_=experts,
                                                 in_offset=bass.IndirectOffsetOnAxis(ap=idx[:, j:j + 1], axis=0)
                                                 ).then_inc(S(f"landed{j % SLOTS}"), 16)

        def x_tile(t):
            return A[:, ds(t * D + X_AT, D)]

        def mod_of(t, kind):
            return A[:, ds((t // LT) * D + (MOD2_AT + kind * 2 * D), D)]

        def norm_act(act, t):
            W(act, "x_out", t)
            nc.scalar.activation(hnext, x_tile(t), ACT.Square, accum_out=s1)
            act.drain()
            nc.scalar.activation(r1, s1, ACT.Sqrt, scale=1.0 / D, bias=eps).then_inc(S("rms"), 1)

        def norm_dve(dve, t):
            W(dve, "rms", t + 1)
            nc.vector.reciprocal(r1, r1)
            dve.drain()
            nc.vector.scalar_tensor_tensor(out=hnext, in0=x_tile(t), scalar=r1, in1=mod_of(t, 1),
                                           op0=ALU.mult, op1=ALU.mult)
            dve.drain()
            nc.vector.tensor_tensor(hnext, hnext, mod_of(t, 0), ALU.add).then_inc(S("hnext"), 1)

        def turn_h(pe, t):
            W(pe, "hnext", t + 1)
            for k in range(KD):
                last = nc.tensor.transpose(hT_ps[:, k * P:(k + 1) * P], hnext[:, k * P:(k + 1) * P], pid)
            last.then_inc(S("hT"), 1)

        def copy_h(act, t):
            W(act, "hT", t + 1)
            nc.scalar.copy(at(PHT_AT, D), hT_ps).then_inc(S("hT_out"), 1)

        def take_h(dve):
            dve.drain()
            return nc.vector.tensor_copy(hcur, hnext)

        def clear_acc(pe, t, last=False):
            if not last:
                W(pe, "acc_free", t + 1)
            for half in range(2):
                mm = nc.tensor.matmul(acc[:, half * 512:(half + 1) * 512], pid, zero.to_broadcast([P, 512]),
                                      start=not last, stop=last, skip_group_check=True)
            return mm

        def pe_tile(pe, t, route):
            clear_acc(pe, t)
            with pe.Fori(0, PEER_HEADS - 1) as h:
                pe_unit(pe, t * PEER_HEADS + h, h + 1, True)
            pe_unit(pe, t * PEER_HEADS + PEER_HEADS - 1, 0, route, first=t + 1)
            clear_acc(pe, t, last=True).then_inc(S("acc"), 1)

        def act_tile(act, t, route):
            if route:
                norm_act(act, t + 1)
            with act.Fori(0, PEER_HEADS - 1) as h:
                act_unit(act, t * PEER_HEADS + h, True)
            act_unit(act, t * PEER_HEADS + PEER_HEADS - 1, route, first=t + 1)

        def dve_tile(dve, t, route):
            with dve.Fori(0, PEER_HEADS - 1) as h:
                dve_unit(dve, t * PEER_HEADS + h, True)
            if route:
                norm_dve(dve, t + 1)
            dve_unit(dve, t * PEER_HEADS + PEER_HEADS - 1, route)
            if route:
                take_h(dve)
            dve.drain()
            W(dve, "acc", t + 1)
            nc.vector.tensor_tensor(hnext, acc, mod_of(t, 2), ALU.mult).then_inc(S("acc_free"), 1)
            dve.drain()
            nc.vector.tensor_tensor(x_tile(t), x_tile(t), hnext, ALU.add).then_inc(S("x_out"), 1)

        with nc.Block() as block:
            @block.sync
            def _(sp):
                sp.dma_start(pid, ident).then_inc(S("tables"), 16)
                sp.dma_start(iota_sb, iota).then_inc(S("tables"), 16)
                sp.dma_start(keys, keys_t[layer]).then_inc(S("keys"), 16)
                for h in range(PEER_HEADS):
                    W(sp, "wq", 16 * h)
                    sp.dma_start(wq.rearrange("p (k n) -> p k n", k=KD)[:, :, h * 256:(h + 1) * 256],
                                 peer_wq[layer].rearrange("(k p) n -> p k n", p=P)[:, :, h * 256:(h + 1) * 256]
                                 ).then_inc(S("wq"), 16)

            @block.gpsimd
            def _(pool):
                pool.sem_inc(S("slots_free"), AHEAD)
                with pool.Fori(0, tiles) as t:
                    with pool.Fori(0, PEER_HEADS, 2) as h:
                        pool_unit(pool, t * PEER_HEADS + h, 0)
                        pool_unit(pool, t * PEER_HEADS + h + 1, 1)

            @block.tensor
            def _(pe):
                W(pe, "tables", 32)
                turn_h(pe, 0)
                W(pe, "hT_out", 1)
                q_product(pe, 0, 0)
                q_turn(pe, 0)
                W(pe, "keys", 16)
                key_product(pe, 0, 0)
                if tiles > 1:
                    with pe.Fori(0, tiles - 1) as t:
                        pe_tile(pe, t, True)
                pe_tile(pe, tiles - 1, False)

            @block.scalar
            def _(act):
                norm_act(act, 0)
                copy_h(act, 0)
                copy_q(act, 0)
                copy_qT(act, 0)
                gate_exp(act, 0)
                with act.Fori(0, tiles - 1) as t:
                    act_tile(act, t, True)
                act_tile(act, tiles - 1, False)

            @block.vector
            def _(dve):
                nc.vector.memset(zero, 0.0)
                W(dve, "tables", 32)
                dve.drain().then_inc(S("acc_free"), 1)
                norm_dve(dve, 0)
                take_h(dve).then_inc(S("x_out"), 1)
                top_keys(dve, 0)
                top_pairs(dve, 0)
                expert_numbers(dve, 0)
                gates(dve, 0)
                with dve.Fori(0, tiles - 1) as t:
                    dve_tile(dve, t, True)
                dve_tile(dve, tiles - 1, False)

    def last_norm():
        g = at(H_AT, D)
        y = at(H_AT + D, LT, D)
        with nc.Block() as block:
            @block.sync
            def _(sp):
                sp.dma_start(g, final_g.to_broadcast([P, D])).then_inc(sem("final_g_in"), 16)
                for t in range(LT):
                    sp.wait_ge(sem("l_done"), t + 1)
                    sp.dma_start(out[t * P:(t + 1) * P, :], y[:, t, :]).then_inc(sem("stored"), 16)
                sp.wait_ge(sem("stored"), 16 * LT)

            @block.scalar
            def _(act):
                square_sums(LT, at(TMP_AT - D, D), "l_rms")

            @block.vector
            def _(dve):
                dve.wait_ge(sem("final_g_in"), 16)
                dve.wait_ge(sem("l_rms"), 1)
                nc.vector.reciprocal(rstd[:, 0:LT], rstd[:, 0:LT])
                dve.drain()
                for t in range(LT):
                    nc.vector.scalar_tensor_tensor(out=y[:, t, :], in0=X[:, t, :], scalar=rstd[:, t:t + 1], in1=g,
                                                   op0=ALU.mult, op1=ALU.mult).then_inc(sem("l_done"), 1)

    modulation(0)
    fourier_layer()
    peer(0, NT)
    modulation(1)
    attention_layer()
    peer(1, LT)
    last_norm()


def kernel(**inputs):
    import numpy as np
    import concourse.bacc as bacc
    from concourse.bass_utils import run_bass_kernel_spmd

    g = {k: np.asarray(v) for k, v in inputs.items()}

    def dft(n, m, norm):
        a = 2.0 * np.pi * ((np.arange(n)[:, None] * np.arange(m)[None, :]) % n) / n
        return np.cos(a) * norm, np.sin(a) * norm

    def token_table(n):
        t = np.stack(dft(n, n, 1.0 / np.sqrt(n * (D // GROUPS))))
        return np.ascontiguousarray(t.reshape(2, n // P, P, n).transpose(2, 0, 1, 3).reshape(P, -1)).astype(np.float32)

    cg, sg = dft(P, P, 1.0)
    dft_g = np.concatenate([cg, -sg], 1).astype(np.float32)
    nf = HEAD_DIM // 4
    freqs = np.float32(ROPE_BASE) ** (-np.arange(nf, dtype=np.float32) / np.float32(nf))
    pos = np.arange(SEQ)
    row = (pos // GRID_W).astype(np.float32)[:, None] * freqs
    col = (pos % GRID_W).astype(np.float32)[:, None] * freqs
    cos = np.concatenate([np.cos(row)] * 2 + [np.cos(col)] * 2, 1)
    sin = np.concatenate([-np.sin(row), np.sin(row), -np.sin(col), np.sin(col)], 1)
    rope = np.stack([cos, sin], 1).reshape(LT, P, 128).transpose(1, 0, 2).reshape(P, -1).astype(np.float32)
    sel = np.zeros((2, 2, P), np.float32)
    sel[0, 0] = sel[1, 1] = 1.0

    arrays = {
        "x": np.concatenate([g["x"][0], g["ctx"][0]], 0),
        "cc": np.stack([g["c"][0], g["c_ctx"]], 1).reshape(KD, P, 2).transpose(1, 0, 2).reshape(P, 2 * KD),
        "w_mod": g["w_mod"], "b_mod": g["b_mod"], "norm_g": g["norm_g"], "four_w": g["four_w_out"][0],
        "diff_w_in": g["diff_w_in"][0], "diff_lam": g["diff_lam"].reshape(1, -1), "diff_g": g["diff_norm_g"],
        "diff_w_out": g["diff_w_out"][0], "peer_wq": g["peer_wq"],
        "keys_t": g["peer_keys"].transpose(0, 4, 1, 2, 3).reshape(2, P, -1),
        "experts": np.concatenate([g["peer_u"], g["peer_v"]], 2).reshape(2 * EXPERTS, 2 * D),
        "final_g": g["final_g"][None, :],
        "dft_l": token_table(SEQ), "dft_c": token_table(CTX), "dft_g": dft_g, "rope": rope,
        "sel": sel.reshape(2, 2 * P), "ident": np.eye(P, dtype=np.float32),
        "iota": np.tile(np.arange(TOPK, dtype=np.float32), (P, 1)),
    }
    arrays = {k: np.ascontiguousarray(v) for k, v in arrays.items()}
    nc = bacc.Bacc("TRN2", target_bir_lowering=False, num_devices=1)
    t = {k: nc.dram_tensor(k, v.shape, mybir.dt.from_np(v.dtype), kind="ExternalInput").ap() for k, v in arrays.items()}
    out = nc.dram_tensor("out", (SEQ, D), mybir.dt.float32, kind="ExternalOutput").ap()
    build(nc, t["x"], t["cc"], t["w_mod"], t["b_mod"], t["norm_g"], t["four_w"], t["diff_w_in"], t["diff_lam"],
          t["diff_g"], t["diff_w_out"], t["peer_wq"], t["keys_t"], t["experts"], t["final_g"], t["dft_l"], t["dft_c"],
          t["dft_g"], (t["rope"], t["sel"]), t["ident"], t["iota"], out)
    r = run_bass_kernel_spmd(nc, [arrays], core_ids=[0])
    return r.results[0]["out"].reshape(1, SEQ, D)
```

```python
import concourse.bass as bass
from concourse import mybir

P = 128
D = 1024
KD = D // P
SEQ, CTX = 512, 256
LT, CT = SEQ // P, CTX // P
NT = LT + CT
GRID_W = 64
GROUPS = 8
HEADS, HEAD_DIM = 8, 64
ROPE_BASE = 10000.0
PEER_HEADS = 8
N_KEYS = 128
EXPERTS = N_KEYS * N_KEYS
TOPK = 16
EPS = 1e-6
LAM_INIT = 0.8 - 0.6 * 0.7408182206817179
SLOTS = 8
BATCH = 2
BATCHES = TOPK // BATCH
AHEAD = SLOTS // BATCH
LOWEST = -3.0e38
EARLY = 4
LATE = 12 - EARLY

X_AT = 0
MOD2_AT = 6144
MOD1_AT = 12288
H_AT = 18432
DFT_L_AT = 24576
DFT_G_AT = 28672
SEL_AT = 30000
RES_AT = 28928
IDENT_AT = 30824
NORM_G_AT = 30952
ROW_AT = 33000
BIAS_AT = 34536
WMOD_AT = 36584
EACC_AT = 19456
E1_AT = 36584
EONES_AT = 21504
YT_AT = 34536
WOUT_AT = 40680
AB_AT = 48872
DFT_C_AT = 51944
LATE_W0_AT = 44776
LATE_A0_AT = 30952
LATE_B0_AT = 33000
LATE_G0_AT = 31976
LATE_ONES0_AT = 30256
LATE_W1_AT = 12288
LATE_A1_AT = 7168
LATE_G1_AT = 9216
LATE_ONES1_AT = 11264
HT_AT = 18432
V_AT = 24576
KT_AT = 30952
QT_AT = 37096
WIN_AT = 41192
ROPE_AT = 49384
ROT_AT = 49896
PROB_AT = 18432
WO_AT = 41192
SUBG_AT = 49384
PROBT_AT = 49896
PROBT2_AT = 12288
YTMP_AT = 15360
ROOT_AT = 23232
TMP_AT = 51944
ONES_AT = 23040
FROM_ROW_AT = 17408
HCUR_AT = 12288
HNEXT_AT = 13312
PHT_AT = 14336
DIAG_AT = 15360
QT1_AT = 16384
CAND_AT = 16640
IDX_AT = 17152
PIDENT_AT = 17664
SMALL_AT = 17792
KEYS_AT = 18152
WQ_AT = 20200
RING_AT = 36584
PERS_AT = 52968
ARENA = 53200


def build(nc, x, cc, w_mod, b_mod, norm_g, four_w, diff_w_in, diff_lam, diff_g, diff_w_out, peer_wq,
          keys_t, experts, final_g, dft_l, dft_c, dft_g, rope, sel, ident, iota, out):
    F32, U32 = mybir.dt.float32, mybir.dt.uint32
    ALU, ACT, AX = mybir.AluOpType, mybir.ActivationFunctionType, mybir.AxisListType
    ds = bass.ds

    A = nc.alloc_sbuf_tensor("arena", [P, ARENA], F32)
    PS = nc.alloc_psum_tensor("ps", [P, 8 * 512], F32)

    def at(off, *shape):
        n = 1
        for s in shape:
            n *= s
        v = A[:, off:off + n]
        if len(shape) == 2:
            v = v.rearrange("p (a b) -> p a b", b=shape[1])
        if len(shape) == 3:
            v = v.rearrange("p (a b c) -> p a b c", b=shape[1], c=shape[2])
        return v

    def bank(b, n=512):
        return PS[:, b * 512:b * 512 + n]

    X = at(X_AT, NT, D)
    ident_sb = at(IDENT_AT, P)
    pers = at(PERS_AT, 232)
    silu_c = pers[:, 0:16].rearrange("p (k s) -> p k s", s=2)
    c_in = pers[:, 16:32]
    ssq = pers[:, 32:40]
    rstd = pers[:, 40:48]
    lam = pers[:, 48:56]
    eps = pers[:, 56:57]
    neg_max = pers[:, 64:68]
    zsum = pers[:, 72:76]
    rz_at = pers[:, 80:84]

    sems = {}

    def sem(name):
        if name not in sems:
            sems[name] = nc.alloc_semaphore(name)
        return sems[name]

    def wait(eng, name, value):
        if not (isinstance(value, int) and value <= 0):
            eng.wait_ge(sem(name), value)

    def mod_row(base, kind, stream):
        return at(base + kind * 2 * D + stream * D, D)

    def square_sums(tiles, junk, signal):
        for t in range(tiles):
            nc.scalar.activation(junk, X[:, t, :], ACT.Square, accum_out=ssq[:, t:t + 1])
            nc.scalar.drain()
        nc.scalar.activation(rstd[:, 0:tiles], ssq[:, 0:tiles], ACT.Sqrt, scale=1.0 / D, bias=eps
                             ).then_inc(sem(signal), 1)

    def modulation(i):
        n = f"m{i}_"
        wm = w_mod[i].rearrange("(k p) n -> p k n", p=P)
        gains = at(NORM_G_AT if i == 0 else E1_AT, D)
        bias = at(BIAS_AT if i == 0 else E1_AT + D, 2 * D)
        acc_at = EACC_AT if i == 0 else E1_AT + 3 * D
        row_at = ROW_AT if i == 0 else E1_AT + 5 * D
        junk = at(H_AT if i == 0 else E1_AT + 7 * D, D)
        ones = at(EONES_AT if i == 0 else E1_AT + 8 * D, P)
        sel_sb = at(SEL_AT if i == 0 else E1_AT + 8 * D + P, 2 * P)[0:2, :]

        def weights(ch):
            return at((WMOD_AT if i == 0 else WQ_AT) + 4096 * ch, KD, 512)

        def row(ch):
            return at(row_at + 512 * ch, 512)[0:2, :]

        def acc(ch, s):
            return at(acc_at + 1024 * (ch // 2) + 512 * s, 512)

        with nc.Block() as block:
            @block.sync
            def _(sp):
                if i == 0:
                    sp.dma_start(c_in, cc).then_inc(sem("c_in"), 16)
                for ch in range(EARLY):
                    if i == 0:
                        sp.dma_start(weights(ch), wm[:, :, ch * 512:(ch + 1) * 512]).then_inc(sem(n + f"w{ch}"), 16)
                    if ch == 1:
                        sp.dma_start(bias[0:2, :], b_mod[i:i + 1, 0:2 * D].to_broadcast([2, 2 * D])
                                     ).then_inc(sem(n + "tables"), 16)
                        sp.dma_start(sel_sb, sel).then_inc(sem(n + "tables"), 16)
                        sp.dma_start(gains, norm_g[i:i + 1, 0, :].to_broadcast([P, D])).then_inc(sem(n + "gains"), 16)
                if i == 0:
                    xt = x.rearrange("(t p) d -> p t d", p=P)
                    sp.dma_start(X[:, 0:LT, :], xt[:, 0:LT, :]).then_inc(sem("x_in"), 16)
                    sp.dma_start(X[:, LT:, :], xt[:, LT:, :]).then_inc(sem("x_in"), 16)
                    sp.dma_start(at(DFT_L_AT, 4096), dft_l).then_inc(sem("dft_in"), 16)
                    sp.dma_start(at(DFT_G_AT, 256), dft_g).then_inc(sem("dft_in"), 16)

            @block.tensor
            def _(pe):
                pe.wait_ge(sem("silu"), 1)

                def product(ch):
                    pe.wait_ge(sem(n + f"w{ch}"), 16)
                    for k in range(KD):
                        last = nc.tensor.matmul(bank(ch // 2)[0:2, :], silu_c[:, k, :], weights(ch)[:, k, :],
                                                start=(k == 0), stop=(k == KD - 1))
                    last.then_inc(sem(n + "product"), 1)

                def spread(ch):
                    wait(pe, n + "spread_out", ch - 1)
                    for s in range(2):
                        o = bank(2 + 2 * (ch % 2) + s)
                        if ch % 2:
                            last = nc.tensor.matmul(o, ones, acc(ch, s), start=True, stop=True)
                        else:
                            last = nc.tensor.matmul(o, sel_sb[:, s * P:(s + 1) * P], row(ch), start=True, stop=True)
                    last.then_inc(sem(n + "spread"), 1)

                for ch in range(0, EARLY, 2):
                    product(ch)
                pe.wait_ge(sem(n + "tables"), 32)
                for ch in range(0, EARLY, 2):
                    pe.wait_ge(sem(n + "row"), ch // 2 + 1)
                    spread(ch)
                    pe.wait_ge(sem(n + "acc"), ch // 2 + 1)
                    spread(ch + 1)

            @block.vector
            def _(dve):
                if i == 0:
                    nc.vector.memset(eps, EPS).then_inc(sem("eps"), 1)
                nc.vector.memset(ones, 1.0)
                dve.wait_ge(sem("silu"), 1)
                for ch in range(0, EARLY, 2):
                    dve.wait_ge(sem(n + f"w{ch + 1}"), 16)
                    for k in range(KD):
                        for s in range(2):
                            a, c, w = acc(ch + 1, s), silu_c[:, k, s:s + 1], weights(ch + 1)[:, k, :]
                            if k == 0:
                                nc.vector.tensor_scalar(a, w, c, None, ALU.mult)
                            else:
                                nc.vector.scalar_tensor_tensor(out=a, in0=w, scalar=c, in1=a, op0=ALU.mult, op1=ALU.add)
                        dve.drain()
                    dve.wait_ge(sem(n + "tables"), 32)
                    dve.wait_ge(sem(n + "product"), ch // 2 + 1)
                    nc.vector.tensor_tensor(row(ch), bank(ch // 2)[0:2, :], bias[0:2, ch * 512:(ch + 1) * 512],
                                            ALU.add).then_inc(sem(n + "row"), 1)
                    for s in range(2):
                        a = acc(ch + 1, s)[0:1, :]
                        last = nc.vector.tensor_tensor(a, a, bias[0:1, (ch + 1) * 512:(ch + 2) * 512], ALU.add)
                    last.then_inc(sem(n + "acc"), 1)
                dve.wait_ge(sem(n + "rms"), 1)
                nc.vector.reciprocal(rstd[:, 0:NT], rstd[:, 0:NT])
                dve.wait_ge(sem(n + "gains"), 16)
                for half in range(2):
                    dve.wait_ge(sem(n + "spread_out"), EARLY - 1 + half)
                    for s in range(2):
                        v = mod_row(MOD1_AT, 1, s)[:, half * 512:(half + 1) * 512]
                        nc.vector.scalar_tensor_tensor(out=v, in0=v, scalar=1.0, op0=ALU.add, op1=ALU.mult,
                                                       in1=gains[:, half * 512:(half + 1) * 512])

            @block.scalar
            def _(act):
                def spread_out(ch):
                    act.wait_ge(sem(n + "spread"), ch + 1)
                    for s in range(2):
                        last = nc.scalar.copy(at(MOD1_AT + ch // 2 * 2 * D + s * D + ch % 2 * 512, 512),
                                              bank(2 + 2 * (ch % 2) + s))
                    last.then_inc(sem(n + "spread_out"), 1)

                if i == 0:
                    act.wait_ge(sem("c_in"), 16)
                    nc.scalar.activation(silu_c.rearrange("p k s -> p (k s)"), c_in, ACT.Silu
                                         ).then_inc(sem("silu"), 1)
                    act.wait_ge(sem("eps"), 1)
                else:
                    square_sums(NT, junk, n + "rms")
                for ch in range(EARLY):
                    spread_out(ch)
                    if i == 0 and ch == 2:
                        act.wait_ge(sem("x_in"), 32)
                        square_sums(NT, junk, n + "rms")

    def late_streams(i):
        return 2 if i == 0 else 1

    def late_place(ch, s):
        kind, half = ch // 2, ch % 2
        return at((MOD1_AT if kind < 3 else MOD2_AT) + (kind % 3) * 2 * D + s * D + half * 512, 512)

    BESIDE = LATE - 2

    def late_bank(i, j, s):
        return bank((3 if i == 0 and j >= BESIDE else 5) + s)

    def late_weights(i, q):
        if i == 0 and q >= 2 * BESIDE:
            return at(H_AT + 2048 * (q % 2), KD // 2, 512)
        return at((LATE_W0_AT if i == 0 else LATE_W1_AT) + 2048 * (q % 2), KD // 2, 512)

    def late_acc(i, j, s):
        return at(((LATE_A0_AT, LATE_B0_AT) if i == 0 else (LATE_A1_AT, LATE_A1_AT + 512))[j % 2] + 512 * s, 512)

    def late_ones(i):
        return at(LATE_ONES0_AT if i == 0 else LATE_ONES1_AT, P)

    def late_gain(i):
        return at(LATE_G0_AT if i == 0 else LATE_G1_AT, D)

    def late_load(eng, i, first=0, end=2 * LATE):
        n = f"m{i}_late_"
        for q in range(first, end):
            ch, k0 = EARLY + q // 2, q % 2 * (KD // 2)
            wait(eng, n + "used", q - 1)
            eng.dma_start(late_weights(i, q), w_mod[i].rearrange("(k p) n -> p k n", p=P)[
                :, k0:k0 + KD // 2, ch * 512:(ch + 1) * 512]).then_inc(sem(n + f"w{q % 2}"), 16)
            if q != 1:
                continue
            eng.dma_start(late_gain(i), norm_g[i:i + 1, 1, :].to_broadcast([P, D])).then_inc(sem(n + "bias"), 16)
            for kind in range(2, 6):
                for s in range(late_streams(i)):
                    eng.dma_start(at((MOD1_AT if kind < 3 else MOD2_AT) + (kind % 3) * 2 * D + s * D, D),
                                  b_mod[i:i + 1, kind * D:(kind + 1) * D].to_broadcast([P, D])
                                  ).then_inc(sem(n + "bias"), 16)

    def late_sum(dve, i, q):
        n = f"m{i}_late_"
        j, k0 = q // 2, q % 2 * (KD // 2)
        w = late_weights(i, q)
        dve.wait_ge(sem(n + f"w{q % 2}"), 16 * (q // 2 + 1))
        if q % 2 == 0:
            wait(dve, n + "spread", j - 1)
        for k in range(KD // 2):
            for s in range(late_streams(i)):
                a, c = late_acc(i, j, s), silu_c[:, k0 + k, s:s + 1]
                if k0 + k == 0:
                    last = nc.vector.tensor_scalar(a, w[:, k, :], c, None, ALU.mult)
                else:
                    last = nc.vector.scalar_tensor_tensor(out=a, in0=w[:, k, :], scalar=c, in1=a,
                                                          op0=ALU.mult, op1=ALU.add)
            if k < KD // 2 - 1:
                dve.drain()
        last.then_inc(sem(n + "used"), 1)
        last = dve.drain()
        if q % 2:
            last.then_inc(sem(n + "sum"), 1)

    def late_spread(pe, i, j):
        n = f"m{i}_late_"
        pe.wait_ge(sem(n + "sum"), j + 1)
        wait(pe, n + "read", j)
        for s in range(late_streams(i)):
            last = nc.tensor.matmul(late_bank(i, j, s), late_ones(i), late_acc(i, j, s), start=True, stop=True)
        last.then_inc(sem(n + "spread"), 1)

    def late_out(dve, i, j):
        n = f"m{i}_late_"
        ch = EARLY + j
        if j == 0:
            dve.wait_ge(sem(n + "bias"), 16 * (1 + 4 * late_streams(i)))
        dve.wait_ge(sem(n + "spread"), j + 1)
        for s in range(late_streams(i)):
            last = nc.vector.tensor_tensor(late_place(ch, s), late_place(ch, s), late_bank(i, j, s), ALU.add)
        last.then_inc(sem(n + "read"), 1)
        if ch // 2 == 4:
            dve.drain()
            for s in range(late_streams(i)):
                nc.vector.scalar_tensor_tensor(out=late_place(ch, s), in0=late_place(ch, s), scalar=1.0,
                                               in1=late_gain(i)[:, ch % 2 * 512:(ch % 2 + 1) * 512],
                                               op0=ALU.add, op1=ALU.mult)


    def fourier_layer():
        H = at(H_AT, NT, D)
        dftL = at(DFT_L_AT, 2, LT, 512)
        dftC = at(DFT_C_AT, 2, CT, 256)
        dftG = at(DFT_G_AT, 2, P)
        wout = at(WOUT_AT, KD, D)
        YT = at(YT_AT, GROUPS, SEQ + CTX)
        res = at(RES_AT, D)

        def chan_out(act, g):
            act.wait_ge(sem("f_chan"), g + 1)
            nc.scalar.copy(YT[:, g, 0:SEQ], bank(3))
            nc.scalar.copy(YT[:, g, SEQ:], bank(4, 256)).then_inc(sem("f_chan_out"), 1)

        with nc.Block() as block:
            @block.sync
            def _(sp):
                sp.dma_start(at(DFT_C_AT, 1024), dft_c).then_inc(sem("dft_in"), 16)
                four = four_w.rearrange("(k p) n -> p k n", p=P)
                late_load(sp, 0, 0, 2 * BESIDE)
                sp.dma_start(wout[:, 0:KD // 2, :], four[:, 0:KD // 2, :]).then_inc(sem("wout_in"), 16)
                sp.wait_ge(sem("m0_late_used"), 2 * BESIDE)
                sp.wait_ge(sem("wout_in"), 16)
                sp.dma_start(wout[:, KD // 2:, :], four[:, KD // 2:, :]).then_inc(sem("wout_in"), 16)
                sp.wait_ge(sem("f_token"), GROUPS)
                late_load(sp, 0, 2 * BESIDE)

            @block.scalar
            def _(act):
                for g in range(GROUPS):
                    act.wait_ge(sem("f_token"), g + 1)
                    wait(act, "f_chan", g - 1)
                    ab = at(AB_AT + 1536 * (g % 2), 2, 768)
                    nc.scalar.copy(ab[:, 0, 0:SEQ], bank(0))
                    nc.scalar.copy(ab[:, 1, 0:SEQ], bank(1))
                    nc.scalar.copy(ab[:, 0, SEQ:], bank(2, 256))
                    nc.scalar.copy(ab[:, 1, SEQ:], bank(7, 256)).then_inc(sem("f_parts"), 1)
                    if g >= 1:
                        chan_out(act, g - 1)
                chan_out(act, GROUPS - 1)

            @block.vector
            def _(dve):
                nc.vector.memset(late_ones(0), 1.0)
                for t in range(NT):
                    s = t // LT
                    nc.vector.scalar_tensor_tensor(out=H[:, t, :], in0=X[:, t, :], scalar=rstd[:, t:t + 1],
                                                   in1=mod_row(MOD1_AT, 1, s), op0=ALU.mult, op1=ALU.mult)
                    dve.drain()
                    nc.vector.tensor_tensor(H[:, t, :], H[:, t, :], mod_row(MOD1_AT, 0, s), ALU.add
                                            ).then_inc(sem("f_norm"), 1)
                for j in range(BESIDE):
                    late_sum(dve, 0, 2 * j)
                    if j >= 1:
                        late_out(dve, 0, j - 1)
                    late_sum(dve, 0, 2 * j + 1)
                late_out(dve, 0, BESIDE - 1)
                dve.drain()
                for t in range(NT):
                    if t < 2:
                        late_sum(dve, 0, 2 * (BESIDE + t))
                        late_sum(dve, 0, 2 * (BESIDE + t) + 1)
                    if t in (2, 4):
                        late_out(dve, 0, BESIDE + t // 2 - 1)
                    dve.wait_ge(sem("f_out"), t + 1)
                    nc.vector.tensor_tensor(res, PS[:, 512 * (5 if t % 2 else 0):][:, 0:D],
                                            mod_row(MOD1_AT, 2, t // LT), ALU.mult).then_inc(sem("f_out_read"), 1)
                    dve.drain()
                    nc.vector.tensor_tensor(X[:, t, :], X[:, t, :], res, ALU.add)
                    dve.drain()

            @block.tensor
            def _(pe):
                def token_transform(g):
                    wait(pe, "f_parts", g)
                    for tab in range(2):
                        for k in range(LT):
                            nc.tensor.matmul(bank(tab), H[:, k, g * P:(g + 1) * P], dftL[:, tab, k, :],
                                             start=(k == 0), stop=(k == LT - 1))
                    if g == 0:
                        pe.wait_ge(sem("f_norm"), NT)
                    for tab in range(2):
                        for k in range(CT):
                            last = nc.tensor.matmul(bank(7 if tab else 2, 256),
                                                    H[:, LT + k, g * P:(g + 1) * P], dftC[:, tab, k, :],
                                                    start=(k == 0), stop=(k == CT - 1))
                    last.then_inc(sem("f_token"), 1)

                def channel_transform(g):
                    pe.wait_ge(sem("f_parts"), g + 1)
                    wait(pe, "f_chan_out", g)
                    ab = at(AB_AT + 1536 * (g % 2), 2, 768)
                    for o, lo, hi in ((bank(3), 0, SEQ), (bank(4, 256), SEQ, SEQ + CTX)):
                        for tab in range(2):
                            last = nc.tensor.matmul(o, dftG[:, tab, :], ab[:, tab, lo:hi],
                                                    start=(tab == 0), stop=(tab == 1))
                    last.then_inc(sem("f_chan"), 1)

                pe.wait_ge(sem("f_norm"), LT)
                pe.wait_ge(sem("dft_in"), 48)
                for g in range(GROUPS):
                    token_transform(g)
                    if g >= 1:
                        channel_transform(g - 1)
                    if g >= 2:
                        late_spread(pe, 0, g - 2)
                channel_transform(GROUPS - 1)
                pe.wait_ge(sem("wout_in"), 16)
                pe.wait_ge(sem("f_chan_out"), GROUPS)
                for t in range(NT):
                    wait(pe, "f_out_read", t - 1)
                    b = 5 if t % 2 else 0
                    if t == 1:
                        pe.wait_ge(sem("m0_late_read"), BESIDE)
                    for part in range(2):
                        if t == 0 and part == 1:
                            pe.wait_ge(sem("wout_in"), 32)
                        for half in range(2):
                            for k in range(part * KD // 2, (part + 1) * KD // 2):
                                last = nc.tensor.matmul(bank(b + half), YT[:, k, t * P:(t + 1) * P],
                                                        wout[:, k, half * 512:(half + 1) * 512],
                                                        start=(k == 0), stop=(k == KD - 1), skip_group_check=True)
                    last.then_inc(sem("f_out"), 1)
                    if t in (1, 3):
                        late_spread(pe, 0, BESIDE + t // 2)

    def attention_layer():
        HT = at(HT_AT, NT, KD, P)
        V = at(V_AT, NT, D)
        KT = at(KT_AT, HEADS, SEQ + CTX)
        QT = at(QT_AT, HEADS, SEQ)
        htmp = at(V_AT, 2, D)
        rope_sb = at(ROPE_AT, LT, 2, 64)
        w_in = diff_w_in.rearrange("(k p) n -> p k n", p=P)
        QCH = [(0, LT), (1, LT), (2, NT), (3, NT), (4, NT), (5, NT)]
        STEPS = [(c, t) for c, n in QCH for t in range(n)]

        with nc.Block() as block:
            @block.sync
            def _(sp):
                sp.dma_start(at(ROPE_AT, LT * 128), rope).then_inc(sem("rope_in"), 16)
                sp.dma_start(ident_sb, ident).then_inc(sem("ident_in"), 16)
                for c in range(2):
                    sp.dma_start(at(WIN_AT + 4096 * c, KD, 512), w_in[:, :, c * 512:(c + 1) * 512]
                                 ).then_inc(sem(f"win{c}"), 16)

                done = 0
                for c, n in QCH:
                    if c >= 2:
                        sp.wait_ge(sem("p_mm"), done)
                        sp.dma_start(at(WIN_AT + 4096 * (c % 2), KD, 512), w_in[:, :, c * 512:(c + 1) * 512]
                                     ).then_inc(sem(f"win{c % 2}"), 16)
                        done += QCH[c - 1][1]
                    else:
                        done = QCH[0][1]

            @block.tensor
            def _(pe):
                def turn(i):
                    pe.wait_ge(sem("p_rot"), i + 1)
                    wait(pe, "p_turn_out", i - 1)
                    for q in range(4):
                        last = nc.tensor.transpose(bank(2 + i % 2)[:, q * P:(q + 1) * P],
                                                   at(ROT_AT + 512 * (i % 2), 512)[:, q * P:(q + 1) * P], ident_sb)
                    last.then_inc(sem("p_turn"), 1)

                def turn_tokens(t):
                    pe.wait_ge(sem("a_norm"), t + 1)
                    wait(pe, "a_tr_out", t - 1)
                    for k in range(KD):
                        last = nc.tensor.transpose(PS[:, (2 + t % 2) * D + k * P:(2 + t % 2) * D + (k + 1) * P],
                                                   htmp[:, t % 2, k * P:(k + 1) * P], ident_sb)
                    last.then_inc(sem("a_tr"), 1)

                pe.wait_ge(sem("ident_in"), 16)
                turn_tokens(0)
                for i, (c, t) in enumerate(STEPS):
                    if i + 1 < NT:
                        turn_tokens(i + 1)
                    if i < NT:
                        pe.wait_ge(sem("a_tr_out"), i + 1)
                    pe.wait_ge(sem(f"win{c % 2}"), 16 * (c // 2 + 1))
                    wait(pe, "p_read", i - 1)
                    w = at(WIN_AT + 4096 * (c % 2), KD, 512)
                    for k in range(KD):
                        last = nc.tensor.matmul(bank(i % 2), HT[:, t, k, :], w[:, k, :],
                                                start=(k == 0), stop=(k == KD - 1))
                    last.then_inc(sem("p_mm"), 1)
                    if i >= 1 and STEPS[i - 1][0] < 4:
                        turn(i - 1)
                    if i >= 8 and i % 2 == 0 and (i - 8) // 2 < LATE:
                        late_spread(pe, 1, (i - 8) // 2)

            @block.gpsimd
            def _(pool):
                pool.wait_ge(sem("a_norm"), NT)
                late_load(pool, 1)

            @block.vector
            def _(dve):
                def norm_tile(t):
                    s = t // LT
                    wait(dve, "a_tr", t - 1)
                    nc.vector.scalar_tensor_tensor(out=htmp[:, t % 2, :], in0=X[:, t, :], scalar=rstd[:, t:t + 1],
                                                   in1=mod_row(MOD1_AT, 1, s), op0=ALU.mult, op1=ALU.mult)
                    dve.drain()
                    nc.vector.tensor_tensor(htmp[:, t % 2, :], htmp[:, t % 2, :], mod_row(MOD1_AT, 0, s), ALU.add
                                            ).then_inc(sem("a_norm"), 1)

                nc.vector.memset(late_ones(1), 1.0)
                norm_tile(0)
                norm_tile(1)
                dve.wait_ge(sem("rope_in"), 16)
                for i, (c, t) in enumerate(STEPS):
                    if i + 2 < NT:
                        norm_tile(i + 2)
                    if 6 <= i < 6 + 2 * LATE:
                        late_sum(dve, 1, i - 6)
                    if i >= 9 and i % 2 and (i - 9) // 2 < LATE:
                        late_out(dve, 1, (i - 9) // 2)
                    dve.wait_ge(sem("p_mm"), i + 1)
                    src = bank(i % 2)
                    if c >= 4:
                        nc.vector.tensor_copy(V[:, t, (c - 4) * 512:(c - 3) * 512], src).then_inc(sem("p_read"), 1)
                        continue
                    wait(dve, "p_turn", i - 1)
                    rot = at(ROT_AT + 512 * (i % 2), 512)
                    if t >= LT:
                        nc.vector.tensor_copy(rot, src).then_inc(sem("p_read"), 1)
                        nc.vector.drain().then_inc(sem("p_rot"), 1)
                        continue
                    cos = rope_sb[:, t, 0:1, :].to_broadcast([P, 8, 64])
                    nc.vector.tensor_tensor(rot.rearrange("p (h d) -> p h d", d=64),
                                            src.rearrange("p (h d) -> p h d", d=64), cos, ALU.mult)
                    tmp = at(TMP_AT, 512)
                    t4 = tmp.rearrange("p (h a b f) -> p h a b f", a=2, b=2, f=16)
                    s4 = src.rearrange("p (h a b f) -> p h a b f", a=2, b=2, f=16)
                    sin = rope_sb[:, t, 1, :].rearrange("p (a b f) -> p a b f", a=2, b=2)
                    for a in range(2):
                        for b in range(2):
                            sb_ = sin[:, a, b, :].unsqueeze(1).to_broadcast([P, 8, 16])
                            last = nc.vector.tensor_tensor(t4[:, :, a, b, :], s4[:, :, a, 1 - b, :], sb_, ALU.mult)
                    last.then_inc(sem("p_read"), 1)
                    dve.drain()
                    nc.vector.tensor_tensor(rot, rot, tmp, ALU.add).then_inc(sem("p_rot"), 1)
                    dve.drain()

            @block.scalar
            def _(act):
                def tokens_out(t):
                    act.wait_ge(sem("a_tr"), t + 1)
                    nc.scalar.copy(at(HT_AT + t * D, D), PS[:, (2 + t % 2) * D:(3 + t % 2) * D]
                                   ).then_inc(sem("a_tr_out"), 1)

                tokens_out(0)
                tokens_out(1)
                for i, (c, t) in enumerate(STEPS):
                    if c >= 4:
                        break
                    if i + 2 < NT:
                        tokens_out(i + 2)
                    act.wait_ge(sem("p_turn"), i + 1)
                    dst, h0 = (QT, 4 * c) if c < 2 else (KT, 4 * (c - 2))
                    nc.scalar.copy(dst[:, h0:h0 + 4, t * P:(t + 1) * P],
                                   bank(2 + i % 2).rearrange("p (q n) -> p q n", n=P)).then_inc(sem("p_turn_out"), 1)

        scale = float(HEAD_DIM) ** -0.5
        K = SEQ + CTX
        wo = at(WO_AT, KD, D)
        tmp = at(YTMP_AT, D)
        into_row = at(ONES_AT, HEADS, HEADS)
        from_row = at(FROM_ROW_AT, HEADS, P)[0:HEADS]
        roots = at(ROOT_AT, SEQ)[0:HEADS, :]
        subg = at(SUBG_AT, 1)
        lam_in = at(SUBG_AT + P, 256)
        UNITS = [(h, m) for h in range(HEADS) for m in range(LT)]
        HALF = NT // 2
        MIX_PARTS = [0, 2, 4, 5, 6]
        turn_ps, o_ps = bank(6, HALF * P), bank(7)

        def prob(i):
            return at(PROB_AT + 3 * K * (i % 2), 3, K)

        def score_ps(i):
            return PS[:, 3 * 512 * (i % 2):3 * 512 * (i % 2 + 1)]

        def probT(h):
            return at(PROBT_AT if h % 2 == 0 else PROBT2_AT, NT, SEQ)

        def SQ(h):
            return KT[:, h, 0:SEQ]

        def OT(h):
            return QT[:, h, :]

        with nc.Block() as block:
            @block.sync
            def _(sp):
                sp.dma_start(lam_in, diff_lam.to_broadcast([P, 256])).then_inc(sem("lam_in"), 16)
                sp.dma_start(subg, diff_g.rearrange("a p -> p a")).then_inc(sem("lam_in"), 16)
                sp.dma_start(wo, diff_w_out.rearrange("(k p) n -> p k n", p=P)).then_inc(sem("wo_in"), 16)

            @block.tensor
            def _(pe):
                def scores(i, c):
                    h, m = UNITS[i]
                    if c == 0:
                        wait(pe, "t_exp", i - 1)
                    for lo, hi in (((0, 512), (512, K)) if c == 0 else ((1024 - K, K), (0, 1024 - K))):
                        if (c, lo) == (1, 0):
                            pe.wait_ge(sem("t_shared"), i + 1)
                        last = nc.tensor.matmul(score_ps(i)[:, c * K + lo:c * K + hi],
                                                QT[64 * c:64 * c + 64, h, m * P:(m + 1) * P],
                                                KT[64 * c:64 * c + 64, h, lo:hi], start=True, stop=True)
                    last.then_inc(sem("t_scores" if c else "t_shared"), 1)

                def turn(i, r):
                    if r == 0:
                        pe.wait_ge(sem("t_diff"), i + 1)
                    wait(pe, "t_turn_out", 2 * i + r)
                    for k in range(HALF):
                        last = nc.tensor.transpose(turn_ps[:, k * P:(k + 1) * P],
                                                   prob(i)[:, 2, (HALF * r + k) * P:(HALF * r + k + 1) * P], ident_sb)
                    last.then_inc(sem("t_turn"), 1)

                def mix(h, first, end):
                    if first == 0:
                        pe.wait_ge(sem("t_turn_out"), 2 * LT * (h + 1))
                        wait(pe, "t_oT", h)
                    for k in range(first, end):
                        mm = nc.tensor.matmul(o_ps, V[:, k, h * P:(h + 1) * P], probT(h)[:, k, :],
                                              start=(k == 0), stop=(k == NT - 1))
                    if end == NT:
                        mm.then_inc(sem("t_mix"), 1)

                for i in range(2):
                    for c in range(2):
                        scores(i, c)
                for i, (h, m) in enumerate(UNITS):
                    if i + 2 < len(UNITS):
                        scores(i + 2, 0)
                        scores(i + 2, 1)
                    turn(i, 0)
                    if h > 0:
                        mix(h - 1, MIX_PARTS[m], MIX_PARTS[m + 1])
                    turn(i, 1)
                mix(HEADS - 1, 0, NT)
                for h in range(HEADS):
                    pe.wait_ge(sem("t_sq"), h + 1)
                    last = nc.tensor.matmul(bank(0)[0:HEADS, :], into_row[:, h, :], SQ(h),
                                            start=(h == 0), stop=(h == HEADS - 1))
                last.then_inc(sem("t_sum"), 1)
                pe.wait_ge(sem("t_root"), 1)
                for h in range(HEADS):
                    wait(pe, "t_onorm", h - 1)
                    nc.tensor.matmul(bank(6 + h % 2), from_row[:, h, :], roots, start=True, stop=True
                                     ).then_inc(sem("t_spread"), 1)
                pe.wait_ge(sem("wo_in"), 16)
                pe.wait_ge(sem("t_onorm"), HEADS)
                for m in range(LT):
                    wait(pe, "t_y_out", m - 1)
                    for half in range(2):
                        for h in range(HEADS):
                            last = nc.tensor.matmul(bank(2 * (m % 2) + half), OT(h)[:, m * P:(m + 1) * P],
                                                    wo[:, h, half * 512:(half + 1) * 512],
                                                    start=(h == 0), stop=(h == HEADS - 1))
                    last.then_inc(sem("t_y"), 1)

            @block.scalar
            def _(act):
                def exponentials(i):
                    act.wait_ge(sem("t_max"), i + 1)
                    wait(act, "t_diff", i - 1)
                    for c in range(2):
                        last = nc.scalar.activation(prob(i)[:, c, :], score_ps(i)[:, c * K:(c + 1) * K], ACT.Exp,
                                                    scale=scale,
                                                    bias=neg_max[:, 2 * (i % 2) + c:2 * (i % 2) + c + 1],
                                                    accum_out=zsum[:, 2 * (i % 2) + c:2 * (i % 2) + c + 1])
                    act.drain().then_inc(sem("t_exp"), 1)

                def values_out(h):
                    act.wait_ge(sem("t_mix"), h + 1)
                    nc.scalar.activation(SQ(h), o_ps, ACT.Square).then_inc(sem("t_sq"), 1)
                    nc.scalar.copy(OT(h), o_ps).then_inc(sem("t_oT"), 1)

                act.wait_ge(sem("t_lam_sum"), 1)
                nc.scalar.activation(lam[:, 2:4], lam[:, 0:2], ACT.Exp).then_inc(sem("t_lam_exp"), 1)
                exponentials(0)
                for i, (h, m) in enumerate(UNITS):
                    if m == 0:
                        wait(act, "t_mix", h - 1)
                    for r in range(2):
                        if r == 0 and i + 1 < len(UNITS):
                            exponentials(i + 1)
                        if r == 0 and m == 0 and h > 1:
                            values_out(h - 2)
                        act.wait_ge(sem("t_turn"), 2 * i + r + 1)
                        nc.scalar.copy(probT(h)[:, HALF * r:HALF * (r + 1), m * P:(m + 1) * P],
                                       turn_ps.rearrange("p (k n) -> p k n", n=P)).then_inc(sem("t_turn_out"), 1)
                values_out(HEADS - 2)
                values_out(HEADS - 1)
                act.wait_ge(sem("t_sum"), 1)
                nc.scalar.activation(roots, bank(0)[0:HEADS, :], ACT.Sqrt, scale=1.0 / P, bias=eps[0:HEADS, :]
                                     ).then_inc(sem("t_orms"), 1)

            @block.vector
            def _(dve):
                dve.wait_ge(sem("lam_in"), 32)
                nc.vector.memset(into_row, 0.0)
                dve.drain()
                for h in range(HEADS):
                    nc.vector.memset(into_row[:, h, h:h + 1], 1.0)
                nc.vector.tensor_copy(from_row, ident_sb[0:HEADS, 0:HEADS].unsqueeze(2).to_broadcast([HEADS, HEADS, P]))
                for j in range(2):
                    nc.vector.tensor_tensor_reduce(out=tmp[:, 0:64], in0=lam_in[:, 128 * j:128 * j + 64],
                                                   in1=lam_in[:, 128 * j + 64:128 * j + 128], scale=1.0, scalar=0.0,
                                                   op0=ALU.mult, op1=ALU.add, accum_out=lam[:, j:j + 1])
                    dve.drain()
                nc.vector.tensor_scalar(subg, subg, 1.0 - LAM_INIT, None, ALU.mult).then_inc(sem("t_lam_sum"), 1)
                dve.wait_ge(sem("t_lam_exp"), 1)
                nc.vector.tensor_tensor(lam[:, 4:5], lam[:, 2:3], lam[:, 3:4], ALU.subtract)
                dve.drain()
                nc.vector.tensor_scalar(lam[:, 5:6], lam[:, 4:5], LAM_INIT, None, ALU.add)
                dve.drain()

                def maxima(i):
                    dve.wait_ge(sem("t_scores"), i + 1)
                    nm = neg_max[:, 2 * (i % 2):2 * (i % 2) + 2]
                    nc.vector.reduce_max(nm, score_ps(i).rearrange("p (c n) -> p c n", c=2), AX.X)
                    dve.drain()
                    nc.vector.tensor_scalar(nm, nm, -scale, None, ALU.mult).then_inc(sem("t_max"), 1)

                def difference(i):
                    pr, z, r = prob(i), zsum[:, 2 * (i % 2):2 * (i % 2) + 2], rz_at[:, 2 * (i % 2):2 * (i % 2) + 2]
                    dve.wait_ge(sem("t_exp"), i + 1)
                    wait(dve, "t_turn", 2 * (i - 1))
                    nc.vector.reciprocal(r, z)
                    dve.drain()
                    nc.vector.tensor_scalar(pr[:, 1, :], pr[:, 1, :], r[:, 1:2], lam[:, 5:6], ALU.mult, ALU.mult)
                    dve.drain()
                    nc.vector.scalar_tensor_tensor(out=pr[:, 2, :], in0=pr[:, 0, :], scalar=r[:, 0:1], in1=pr[:, 1, :],
                                                   op0=ALU.mult, op1=ALU.subtract).then_inc(sem("t_diff"), 1)

                maxima(0)
                for i, (h, m) in enumerate(UNITS):
                    if i + 1 < len(UNITS):
                        maxima(i + 1)
                    difference(i)
                dve.wait_ge(sem("t_orms"), 1)
                nc.vector.reciprocal(roots, roots).then_inc(sem("t_root"), 1)
                dve.wait_ge(sem("t_oT"), HEADS)
                for h in range(HEADS):
                    dve.wait_ge(sem("t_spread"), h + 1)
                    nc.vector.scalar_tensor_tensor(out=OT(h), in0=OT(h), scalar=subg, in1=bank(6 + h % 2),
                                                   op0=ALU.mult, op1=ALU.mult).then_inc(sem("t_onorm"), 1)
                for m in range(LT):
                    dve.wait_ge(sem("t_y"), m + 1)
                    nc.vector.tensor_tensor(tmp, PS[:, D * (m % 2):D * (m % 2 + 1)], mod_row(MOD1_AT, 2, 0), ALU.mult
                                            ).then_inc(sem("t_y_out"), 1)
                    dve.drain()
                    nc.vector.tensor_tensor(X[:, m, :], X[:, m, :], tmp, ALU.add)
                    dve.drain()

    def peer(layer, tiles):
        n_ = f"e{layer}_"
        S = lambda name: sem(n_ + name)
        W = lambda eng, name, value: wait(eng, n_ + name, value)

        def wait_apart(eng, name, value):
            W(eng, name, value)
            if not isinstance(value, int):
                eng.sem_inc(sem("seen"), 1)

        hcur, hnext = at(HCUR_AT, D), at(HNEXT_AT, D)
        hT = at(PHT_AT, KD, P)
        diag = at(DIAG_AT, SLOTS, P)
        q_sb, qT = at(CAND_AT, 256), at(QT1_AT, 2, P)
        cand, masked = at(CAND_AT, 256), at(CAND_AT + 256, 256)
        grid2 = at(CAND_AT, 512)
        pid = at(PIDENT_AT, P)
        keys = at(KEYS_AT, 2 * PEER_HEADS * N_KEYS)
        wq = at(WQ_AT, KD * 2048)
        ring = at(RING_AT, SLOTS, 2 * D)
        small = at(SMALL_AT, 360)
        top = small[:, 0:32]
        top_i = small[:, 32:64].bitcast(U32)
        best = small[:, 64:80]
        pos = small[:, 80:112].bitcast(U32)
        rank = small[:, 112:144]
        top_f = small[:, 144:176]
        part = small[:, 176:208]
        shifted = small[:, 208:224]
        expo = small[:, 224:240]
        total = small[:, 240:241]
        rtotal = small[:, 241:242]
        gate_next = small[:, 244:260]
        gate = small[:, 260:276]
        idx_f = small[:, 276:292]
        idx2 = at(IDX_AT, 2 * TOPK).bitcast(U32)
        dots = small[:, 308:324]
        act_out = small[:, 324:340]
        iota_sb = small[:, 340:356]
        r1 = small[:, 356:357]
        s1 = small[:, 357:358]
        zero = small[:, 358:359]
        acc, q_ps, qT_ps, s_ps = PS[:, 0:D], bank(2, 256), bank(3, 256), bank(4, 256)
        hT_ps = PS[:, 5 * 512:5 * 512 + D]

        def q_product(pe, r, head):
            W(pe, "wq", head * 16 + 16)
            for k in range(KD):
                last = nc.tensor.matmul(q_ps, hT[:, k, :], wq[:, ds(head * 256 + k * 2048, 256)],
                                        start=(k == 0), stop=(k == KD - 1))
            last.then_inc(S("q"), 1)

        def q_turn(pe, r):
            W(pe, "q_out", r + 1)
            for c in range(2):
                last = nc.tensor.transpose(qT_ps[:, c * P:(c + 1) * P], q_sb[:, c * P:(c + 1) * P], pid)
            last.then_inc(S("qT"), 1)

        def key_product(pe, r, head):
            W(pe, "qT_out", r + 1)
            for c in range(2):
                last = nc.tensor.matmul(s_ps[:, c * P:(c + 1) * P], qT[:, c, :],
                                        keys[:, ds(head * 256 + c * P, P)], start=True, stop=True)
            last.then_inc(S("scores"), 1)

        def copy_q(act, r):
            W(act, "q", r + 1)
            W(act, "idx", r)
            nc.scalar.copy(q_sb, q_ps).then_inc(S("q_out"), 1)

        def copy_qT(act, r):
            W(act, "qT", r + 1)
            W(act, "scores", r)
            nc.scalar.copy(at(QT1_AT, 256), qT_ps).then_inc(S("qT_out"), 1)

        def gate_exp(act, r):
            W(act, "best", r + 1)
            nc.scalar.activation(expo, shifted, ACT.Exp, accum_out=total)
            act.drain().then_inc(S("expo"), 1)

        def top_keys(dve, r):
            wait_apart(dve, "scores", r + 1)
            for o in (0, 8):
                src = [s_ps[:, 0:P], s_ps[:, P:2 * P]] if o == 0 else [masked[:, 0:P], masked[:, P:2 * P]]
                for c in range(2):
                    nc.vector.max(top[:, 16 * c + o:16 * c + o + 8], src[c])
                dve.drain()
                for c in range(2):
                    nc.vector.max_index(top_i[:, 16 * c + o:16 * c + o + 8], top[:, 16 * c + o:16 * c + o + 8], src[c])
                    if o == 0:
                        nc.vector.match_replace(masked[:, c * P:(c + 1) * P], top[:, 16 * c:16 * c + 8], src[c], LOWEST)
                dve.drain()

        def top_pairs(dve, r):
            nc.vector.tensor_tensor(cand.rearrange("p (a b) -> p a b", b=TOPK),
                                    top[:, 0:16].unsqueeze(2).to_broadcast([P, TOPK, TOPK]),
                                    top[:, 16:32].unsqueeze(1).to_broadcast([P, TOPK, TOPK]), ALU.add)
            nc.vector.tensor_copy(top_f, top_i)
            dve.drain()
            nc.vector.max(best[:, 0:8], cand)
            dve.drain()
            nc.vector.max_index(pos[:, 0:8], best[:, 0:8], cand)
            nc.vector.match_replace(masked, best[:, 0:8], cand, LOWEST)
            dve.drain()
            nc.vector.max(best[:, 8:16], masked)
            dve.drain()
            nc.vector.max_index(pos[:, 8:16], best[:, 8:16], masked)
            nc.vector.tensor_scalar(shifted, best, best[:, 0:1], None, ALU.subtract).then_inc(S("best"), 1)
            dve.drain()

        def expert_numbers(dve, r):
            nc.vector.tensor_scalar(pos[:, 16:32], pos[:, 0:16], 15, None, ALU.bitwise_and)
            dve.drain()
            nc.vector.tensor_scalar(pos[:, 0:16], pos[:, 0:16], 4, None, ALU.logical_shift_right)
            dve.drain()
            nc.vector.tensor_copy(rank, pos)
            dve.drain()
            g3 = grid2.rearrange("p (a b) -> p a b", b=TOPK)
            nc.vector.tensor_tensor(g3, rank.unsqueeze(2).to_broadcast([P, 32, TOPK]),
                                    iota_sb.unsqueeze(1).to_broadcast([P, 32, TOPK]), ALU.is_equal)
            dve.drain()
            for c in range(2):
                nc.vector.tensor_tensor(g3[:, 16 * c:16 * c + 16, :], g3[:, 16 * c:16 * c + 16, :],
                                        top_f[:, 16 * c:16 * c + 16].unsqueeze(1).to_broadcast([P, TOPK, TOPK]),
                                        ALU.mult)
            dve.drain()
            nc.vector.reduce_sum(part, g3, AX.X)
            dve.drain()
            W(dve, "idx_taken", r)
            nc.vector.scalar_tensor_tensor(out=idx_f, in0=part[:, 0:16], scalar=float(N_KEYS), in1=part[:, 16:32],
                                           op0=ALU.mult, op1=ALU.add).then_inc(S("idx"), 1)

        def gates(dve, r):
            W(dve, "expo", r + 1)
            nc.vector.reciprocal(rtotal, total)
            dve.drain()
            nc.vector.tensor_scalar(gate_next, expo, rtotal, None, ALU.mult)

        def pe_unit(pe, u, next_head, route, first=None):
            if route:
                if first is not None:
                    turn_h(pe, first)
                    W(pe, "hT_out", first + 1)
                q_product(pe, u + 1, next_head)
            for b in range(BATCHES):
                W(pe, "diag", u * BATCHES + b + 1)
                for j in range(BATCH):
                    s = (b * BATCH + j) % SLOTS
                    for half in range(2):
                        last = nc.tensor.matmul(acc[:, half * 512:(half + 1) * 512], diag[:, s, :],
                                                ring[:, s, D + half * 512:D + (half + 1) * 512],
                                                start=False, stop=False, skip_group_check=True)
                last.then_inc(S("slots_free"), 1)
                if route and b == 0:
                    q_turn(pe, u + 1)
                if route and b == 1:
                    key_product(pe, u + 1, next_head)

        def act_unit(act, u, route, first=None):
            if route and first is not None:
                copy_h(act, first)
            for b in range(BATCHES):
                W(act, "dots", u * BATCHES + b + 1)
                nc.scalar.activation(act_out[:, b * BATCH:(b + 1) * BATCH], dots[:, b * BATCH:(b + 1) * BATCH],
                                     ACT.Gelu).then_inc(S("gelu"), 1)
                if route and b == 0:
                    copy_q(act, u + 1)
                if route and b == 1:
                    copy_qT(act, u + 1)
                if route and b == 5:
                    gate_exp(act, u + 1)

        def dve_unit(dve, u, route):
            def diagonals(b):
                W(dve, "gelu", u * BATCHES + b + 1)
                for j in range(b * BATCH, (b + 1) * BATCH):
                    last = nc.vector.tensor_scalar(diag[:, j % SLOTS, :], pid, act_out[:, j:j + 1], gate[:, j:j + 1],
                                                   ALU.mult, ALU.mult)
                last.then_inc(S("diag"), 1)

            dve.drain()
            nc.vector.tensor_copy(gate, gate_next)
            dve.drain()
            for b in range(BATCHES):
                for j in range(b * BATCH, (b + 1) * BATCH):
                    W(dve, f"landed{j % SLOTS}", u * 32 + 16 * (j // SLOTS + 1))
                    u_row = ring[:, j % SLOTS, 0:D]
                    last = nc.vector.tensor_tensor_reduce(out=u_row, in0=u_row, in1=hcur, scale=1.0, scalar=0.0,
                                                          op0=ALU.mult, op1=ALU.add, accum_out=dots[:, j:j + 1])
                last.then_inc(S("dots"), 1)
                if b >= 1:
                    diagonals(b - 1)
                if route and b == 3:
                    top_keys(dve, u + 1)
                if route and b == 4:
                    top_pairs(dve, u + 1)
                if route and b == 5:
                    expert_numbers(dve, u + 1)
                if route and b == 6:
                    gates(dve, u + 1)
            diagonals(BATCHES - 1)

        def pool_unit(pool, u, parity):
            idx = idx2[:, parity * TOPK:(parity + 1) * TOPK]
            wait_apart(pool, "idx", u + 1)
            nc.gpsimd.tensor_scalar_add(idx, idx_f, float(layer * EXPERTS)).then_inc(S("idx_taken"), 1)
            wait_apart(pool, "idx_taken", u + 1)
            for b in range(BATCHES):
                wait_apart(pool, "slots_free", u * BATCHES + b + 1)
                for j in range(b * BATCH, (b + 1) * BATCH):
                    nc.gpsimd.indirect_dma_start(out=ring[:, j % SLOTS, :], out_offset=None, in_=experts,
                                                 in_offset=bass.IndirectOffsetOnAxis(ap=idx[:, j:j + 1], axis=0)
                                                 ).then_inc(S(f"landed{j % SLOTS}"), 16)

        def x_tile(t):
            return A[:, ds(t * D + X_AT, D)]

        def mod_of(t, kind):
            return A[:, ds((t // LT) * D + (MOD2_AT + kind * 2 * D), D)]

        def norm_act(act, t):
            W(act, "x_out", t)
            nc.scalar.activation(hnext, x_tile(t), ACT.Square, accum_out=s1)
            act.drain()
            nc.scalar.activation(r1, s1, ACT.Sqrt, scale=1.0 / D, bias=eps).then_inc(S("rms"), 1)

        def norm_dve(dve, t):
            W(dve, "rms", t + 1)
            nc.vector.reciprocal(r1, r1)
            dve.drain()
            nc.vector.scalar_tensor_tensor(out=hnext, in0=x_tile(t), scalar=r1, in1=mod_of(t, 1),
                                           op0=ALU.mult, op1=ALU.mult)
            dve.drain()
            nc.vector.tensor_tensor(hnext, hnext, mod_of(t, 0), ALU.add).then_inc(S("hnext"), 1)

        def turn_h(pe, t):
            W(pe, "hnext", t + 1)
            for k in range(KD):
                last = nc.tensor.transpose(hT_ps[:, k * P:(k + 1) * P], hnext[:, k * P:(k + 1) * P], pid)
            last.then_inc(S("hT"), 1)

        def copy_h(act, t):
            W(act, "hT", t + 1)
            nc.scalar.copy(at(PHT_AT, D), hT_ps).then_inc(S("hT_out"), 1)

        def take_h(dve):
            dve.drain()
            return nc.vector.tensor_copy(hcur, hnext)

        def clear_acc(pe, t, last=False):
            if not last:
                W(pe, "acc_free", t + 1)
            for half in range(2):
                mm = nc.tensor.matmul(acc[:, half * 512:(half + 1) * 512], pid, zero.to_broadcast([P, 512]),
                                      start=not last, stop=last, skip_group_check=True)
            return mm

        def pe_tile(pe, t, route):
            clear_acc(pe, t)
            with pe.Fori(0, PEER_HEADS - 1) as h:
                pe_unit(pe, t * PEER_HEADS + h, h + 1, True)
            pe_unit(pe, t * PEER_HEADS + PEER_HEADS - 1, 0, route, first=t + 1)
            clear_acc(pe, t, last=True).then_inc(S("acc"), 1)

        def act_tile(act, t, route):
            if route:
                norm_act(act, t + 1)
            with act.Fori(0, PEER_HEADS - 1) as h:
                act_unit(act, t * PEER_HEADS + h, True)
            act_unit(act, t * PEER_HEADS + PEER_HEADS - 1, route, first=t + 1)

        def dve_tile(dve, t, route):
            with dve.Fori(0, PEER_HEADS - 1) as h:
                dve_unit(dve, t * PEER_HEADS + h, True)
            if route:
                norm_dve(dve, t + 1)
            dve_unit(dve, t * PEER_HEADS + PEER_HEADS - 1, route)
            if route:
                take_h(dve)
            dve.drain()
            W(dve, "acc", t + 1)
            nc.vector.tensor_tensor(hnext, acc, mod_of(t, 2), ALU.mult).then_inc(S("acc_free"), 1)
            dve.drain()
            nc.vector.tensor_tensor(x_tile(t), x_tile(t), hnext, ALU.add).then_inc(S("x_out"), 1)

        with nc.Block() as block:
            @block.sync
            def _(sp):
                sp.dma_start(pid, ident).then_inc(S("tables"), 16)
                sp.dma_start(iota_sb, iota).then_inc(S("tables"), 16)
                sp.dma_start(keys, keys_t[layer]).then_inc(S("keys"), 16)
                for h in range(PEER_HEADS):
                    W(sp, "wq", 16 * h)
                    sp.dma_start(wq.rearrange("p (k n) -> p k n", k=KD)[:, :, h * 256:(h + 1) * 256],
                                 peer_wq[layer].rearrange("(k p) n -> p k n", p=P)[:, :, h * 256:(h + 1) * 256]
                                 ).then_inc(S("wq"), 16)
                if layer == 0:
                    W(sp, "q", tiles * PEER_HEADS)
                    W(sp, f"landed{SLOTS - 1}", 32 * tiles * PEER_HEADS)
                    for ch in range(EARLY):
                        sp.dma_start(at(WQ_AT + 4096 * ch, KD, 512),
                                     w_mod[1].rearrange("(k p) n -> p k n", p=P)[:, :, ch * 512:(ch + 1) * 512]
                                     ).then_inc(sem(f"m1_w{ch}"), 16)

            @block.gpsimd
            def _(pool):
                pool.sem_inc(S("slots_free"), AHEAD)
                with pool.Fori(0, tiles) as t:
                    with pool.Fori(0, PEER_HEADS, 2) as h:
                        pool_unit(pool, t * PEER_HEADS + h, 0)
                        pool_unit(pool, t * PEER_HEADS + h + 1, 1)

            @block.tensor
            def _(pe):
                W(pe, "tables", 32)
                turn_h(pe, 0)
                W(pe, "hT_out", 1)
                q_product(pe, 0, 0)
                q_turn(pe, 0)
                W(pe, "keys", 16)
                key_product(pe, 0, 0)
                if tiles > 1:
                    with pe.Fori(0, tiles - 1) as t:
                        pe_tile(pe, t, True)
                pe_tile(pe, tiles - 1, False)

            @block.scalar
            def _(act):
                norm_act(act, 0)
                copy_h(act, 0)
                copy_q(act, 0)
                copy_qT(act, 0)
                gate_exp(act, 0)
                with act.Fori(0, tiles - 1) as t:
                    act_tile(act, t, True)
                act_tile(act, tiles - 1, False)

            @block.vector
            def _(dve):
                nc.vector.memset(zero, 0.0)
                W(dve, "tables", 32)
                dve.drain().then_inc(S("acc_free"), 1)
                norm_dve(dve, 0)
                take_h(dve).then_inc(S("x_out"), 1)
                top_keys(dve, 0)
                top_pairs(dve, 0)
                expert_numbers(dve, 0)
                gates(dve, 0)
                with dve.Fori(0, tiles - 1) as t:
                    dve_tile(dve, t, True)
                dve_tile(dve, tiles - 1, False)

    def last_norm():
        g = at(H_AT, D)
        y = at(H_AT + D, LT, D)
        with nc.Block() as block:
            @block.sync
            def _(sp):
                sp.dma_start(g, final_g.to_broadcast([P, D])).then_inc(sem("final_g_in"), 16)
                for t in range(LT):
                    sp.wait_ge(sem("l_done"), t + 1)
                    sp.dma_start(out[t * P:(t + 1) * P, :], y[:, t, :]).then_inc(sem("stored"), 16)
                sp.wait_ge(sem("stored"), 16 * LT)

            @block.scalar
            def _(act):
                square_sums(LT, at(TMP_AT - D, D), "l_rms")

            @block.vector
            def _(dve):
                dve.wait_ge(sem("final_g_in"), 16)
                dve.wait_ge(sem("l_rms"), 1)
                nc.vector.reciprocal(rstd[:, 0:LT], rstd[:, 0:LT])
                dve.drain()
                for t in range(LT):
                    nc.vector.scalar_tensor_tensor(out=y[:, t, :], in0=X[:, t, :], scalar=rstd[:, t:t + 1], in1=g,
                                                   op0=ALU.mult, op1=ALU.mult).then_inc(sem("l_done"), 1)

    modulation(0)
    fourier_layer()
    peer(0, NT)
    modulation(1)
    attention_layer()
    peer(1, LT)
    last_norm()


def kernel(**inputs):
    import numpy as np
    import concourse.bacc as bacc
    from concourse.bass_utils import run_bass_kernel_spmd

    g = {k: np.asarray(v) for k, v in inputs.items()}

    def dft(n, m, norm):
        a = 2.0 * np.pi * ((np.arange(n)[:, None] * np.arange(m)[None, :]) % n) / n
        return np.cos(a) * norm, np.sin(a) * norm

    def token_table(n):
        t = np.stack(dft(n, n, 1.0 / np.sqrt(n * (D // GROUPS))))
        return np.ascontiguousarray(t.reshape(2, n // P, P, n).transpose(2, 0, 1, 3).reshape(P, -1)).astype(np.float32)

    cg, sg = dft(P, P, 1.0)
    dft_g = np.concatenate([cg, -sg], 1).astype(np.float32)
    nf = HEAD_DIM // 4
    freqs = np.float32(ROPE_BASE) ** (-np.arange(nf, dtype=np.float32) / np.float32(nf))
    pos = np.arange(SEQ)
    row = (pos // GRID_W).astype(np.float32)[:, None] * freqs
    col = (pos % GRID_W).astype(np.float32)[:, None] * freqs
    cos = np.concatenate([np.cos(row)] * 2 + [np.cos(col)] * 2, 1)
    sin = np.concatenate([-np.sin(row), np.sin(row), -np.sin(col), np.sin(col)], 1)
    rope = np.stack([cos, sin], 1).reshape(LT, P, 128).transpose(1, 0, 2).reshape(P, -1).astype(np.float32)
    sel = np.zeros((2, 2, P), np.float32)
    sel[0, 0] = sel[1, 1] = 1.0

    arrays = {
        "x": np.concatenate([g["x"][0], g["ctx"][0]], 0),
        "cc": np.stack([g["c"][0], g["c_ctx"]], 1).reshape(KD, P, 2).transpose(1, 0, 2).reshape(P, 2 * KD),
        "w_mod": g["w_mod"], "b_mod": g["b_mod"], "norm_g": g["norm_g"], "four_w": g["four_w_out"][0],
        "diff_w_in": g["diff_w_in"][0], "diff_lam": g["diff_lam"].reshape(1, -1), "diff_g": g["diff_norm_g"],
        "diff_w_out": g["diff_w_out"][0], "peer_wq": g["peer_wq"],
        "keys_t": g["peer_keys"].transpose(0, 4, 1, 2, 3).reshape(2, P, -1),
        "experts": np.concatenate([g["peer_u"], g["peer_v"]], 2).reshape(2 * EXPERTS, 2 * D),
        "final_g": g["final_g"][None, :],
        "dft_l": token_table(SEQ), "dft_c": token_table(CTX), "dft_g": dft_g, "rope": rope,
        "sel": sel.reshape(2, 2 * P), "ident": np.eye(P, dtype=np.float32),
        "iota": np.tile(np.arange(TOPK, dtype=np.float32), (P, 1)),
    }
    arrays = {k: np.ascontiguousarray(v) for k, v in arrays.items()}
    nc = bacc.Bacc("TRN2", target_bir_lowering=False, num_devices=1)
    t = {k: nc.dram_tensor(k, v.shape, mybir.dt.from_np(v.dtype), kind="ExternalInput").ap() for k, v in arrays.items()}
    out = nc.dram_tensor("out", (SEQ, D), mybir.dt.float32, kind="ExternalOutput").ap()
    build(nc, t["x"], t["cc"], t["w_mod"], t["b_mod"], t["norm_g"], t["four_w"], t["diff_w_in"], t["diff_lam"],
          t["diff_g"], t["diff_w_out"], t["peer_wq"], t["keys_t"], t["experts"], t["final_g"], t["dft_l"], t["dft_c"],
          t["dft_g"], t["rope"], t["sel"], t["ident"], t["iota"], out)
    r = run_bass_kernel_spmd(nc, [arrays], core_ids=[0])
    return r.results[0]["out"].reshape(1, SEQ, D)
```
